# Optimizing a Trainium2 kernel written in Bass

```python
import jax, jax.numpy as jnp
from jax import lax
import numpy as np

D_MODEL = 1024
BATCH = 1
SEQ = 256
DEPTH = 2

N_EVEN = (DEPTH + 1) // 2
N_ODD = DEPTH // 2

HEAD_DIM = 64
N_HEADS = D_MODEL // HEAD_DIM
N_KV_HEADS = 4
GROUP = N_HEADS // N_KV_HEADS
Q_WIDTH = N_HEADS * HEAD_DIM
KV_WIDTH = N_KV_HEADS * HEAD_DIM
QKV_WIDTH = Q_WIDTH + 2 * KV_WIDTH
WINDOW = 128
BLOCK = 128
NEG_INF = -1e30

POOL_WINDOWS = (2, 4, 8, 16)
N_POOL_GROUPS = len(POOL_WINDOWS)
POOL_GROUP_DIM = D_MODEL // N_POOL_GROUPS

D_FF = 2816
N_EXPERTS = 8
TOP_K = 2
D_FF_EXPERT = 3584

RMS_EPS = 1e-5

kernel_name = "hybrid_swa_sink_alibi_pool_moe_trunk"

def rms_norm(x, gain):
    xf = x.astype(jnp.float32)
    y = xf * lax.rsqrt(jnp.mean(xf * xf, axis=-1, keepdims=True) + RMS_EPS)
    return (y * gain.astype(jnp.float32)).astype(x.dtype)

def alibi_slopes(n_heads):
    return jnp.exp2(-8.0 * jnp.arange(1, n_heads + 1, dtype=jnp.float32) / n_heads)

def swiglu(h, w_gate, w_up, w_down):
    return (jax.nn.silu(h @ w_gate) * (h @ w_up)) @ w_down

def sliding_window_attention(h, w_qkv, sinks, w_o):
    B, S, _ = h.shape
    nb = S // BLOCK
    qkv = h @ w_qkv
    q, k, v = jnp.split(qkv, [Q_WIDTH, Q_WIDTH + KV_WIDTH], axis=-1)
    q = q.reshape(B, nb, BLOCK, N_KV_HEADS, GROUP, HEAD_DIM)
    k = k.reshape(B, nb, BLOCK, N_KV_HEADS, HEAD_DIM)
    v = v.reshape(B, nb, BLOCK, N_KV_HEADS, HEAD_DIM)

    def with_prev(t):
        prev = jnp.pad(t[:, :-1], ((0, 0), (1, 0), (0, 0), (0, 0), (0, 0)))
        return jnp.concatenate([prev, t], axis=2)

    kb, vb = with_prev(k), with_prev(v)
    s = jnp.einsum('bnqhgd,bnkhd->bhgnqk', q, kb,
                   preferred_element_type=jnp.float32) * (HEAD_DIM ** -0.5)

    blk = jnp.arange(nb)[:, None, None] * BLOCK
    q_pos = blk + jnp.arange(BLOCK)[None, :, None]
    k_pos = blk - BLOCK + jnp.arange(2 * BLOCK)[None, None, :]
    dist = q_pos - k_pos
    valid = (dist >= 0) & (dist < WINDOW) & (k_pos >= 0)
    slopes = alibi_slopes(N_HEADS).reshape(N_KV_HEADS, GROUP)
    bias = -slopes[:, :, None, None, None] * dist.astype(jnp.float32)[None, None]
    s = jnp.where(valid[None, None, None], s + bias[None], NEG_INF)

    sink = jnp.broadcast_to(sinks.astype(jnp.float32).reshape(1, N_KV_HEADS, GROUP, 1, 1, 1),
                            s.shape[:-1] + (1,))
    p = jax.nn.softmax(jnp.concatenate([s, sink], axis=-1), axis=-1)[..., :-1]
    o = jnp.einsum('bhgnqk,bnkhd->bnqhgd', p.astype(vb.dtype), vb)
    return o.reshape(B, S, Q_WIDTH) @ w_o

def pooling_mixer(h, w_pool, scale):
    B, S, D = h.shape
    groups = jnp.split(h, N_POOL_GROUPS, axis=-1)
    count = jnp.arange(1, S + 1, dtype=jnp.float32)[None, :, None]
    outs = []
    for g, w in zip(groups, POOL_WINDOWS):
        gf = g.astype(jnp.float32)
        c = lax.cumsum(gf, axis=1)
        lower = jnp.pad(c[:, :S - w], ((0, 0), (w, 0), (0, 0)))
        mean = (c - lower) / jnp.minimum(count, float(w))
        outs.append((mean - gf).astype(h.dtype))
    p = jnp.stack(outs, axis=2)
    y = jnp.einsum('bsgc,gcd->bsgd', p, w_pool).reshape(B, S, D)
    return y * scale

def moe_swiglu(h, w_router, w_gate, w_up, w_down):
    B, S, D = h.shape
    t = h.reshape(B * S, D)
    logits = jnp.dot(t, w_router, preferred_element_type=jnp.float32)
    top_val, top_idx = lax.top_k(logits, TOP_K)
    gates = jax.nn.softmax(top_val, axis=-1)
    combine = jnp.sum(jax.nn.one_hot(top_idx, N_EXPERTS, dtype=jnp.float32)
                      * gates[..., None], axis=1).astype(t.dtype)
    out = jnp.zeros_like(t)
    for e in range(N_EXPERTS):
        out = out + combine[:, e:e + 1] * swiglu(t, w_gate[e], w_up[e], w_down[e])
    return out.reshape(B, S, D)

def setup_inputs(seed: int = 0) -> dict:
    key = jax.random.key(seed)
    ks = jax.random.split(key, 24)
    f32 = jnp.float32
    nrm = lambda k, shape, scale: jax.random.normal(k, shape, f32) * scale
    gain = lambda k, shape: 1.0 + 0.05 * jax.random.normal(k, shape, f32)
    return {
        "x": jax.random.normal(ks[0], (BATCH, SEQ, D_MODEL), f32),
        "attn_norm": gain(ks[1], (N_EVEN, D_MODEL)),
        "attn_w_qkv": nrm(ks[2], (N_EVEN, D_MODEL, QKV_WIDTH), D_MODEL ** -0.5),
        "attn_sinks": nrm(ks[3], (N_EVEN, N_HEADS), 0.5),
        "attn_w_o": nrm(ks[4], (N_EVEN, Q_WIDTH, D_MODEL), Q_WIDTH ** -0.5),
        "ffn_norm": gain(ks[5], (N_EVEN, D_MODEL)),
        "ffn_w_gate": nrm(ks[6], (N_EVEN, D_MODEL, D_FF), D_MODEL ** -0.5),
        "ffn_w_up": nrm(ks[7], (N_EVEN, D_MODEL, D_FF), D_MODEL ** -0.5),
        "ffn_w_down": nrm(ks[8], (N_EVEN, D_FF, D_MODEL), D_FF ** -0.5),
        "pool_norm": gain(ks[9], (N_ODD, D_MODEL)),
        "pool_w": nrm(ks[10], (N_ODD, N_POOL_GROUPS, POOL_GROUP_DIM, POOL_GROUP_DIM), POOL_GROUP_DIM ** -0.5),
        "pool_scale": gain(ks[11], (N_ODD, D_MODEL)),
        "moe_norm": gain(ks[12], (N_ODD, D_MODEL)),
        "moe_w_router": nrm(ks[13], (N_ODD, D_MODEL, N_EXPERTS), D_MODEL ** -0.5),
        "moe_w_gate": nrm(ks[14], (N_ODD, N_EXPERTS, D_MODEL, D_FF_EXPERT), D_MODEL ** -0.5),
        "moe_w_up": nrm(ks[15], (N_ODD, N_EXPERTS, D_MODEL, D_FF_EXPERT), D_MODEL ** -0.5),
        "moe_w_down": nrm(ks[16], (N_ODD, N_EXPERTS, D_FF_EXPERT, D_MODEL), D_FF_EXPERT ** -0.5),
        "final_norm": gain(ks[17], (D_MODEL,)),
    }

def reference(x, attn_norm, attn_w_qkv, attn_sinks, attn_w_o,
              ffn_norm, ffn_w_gate, ffn_w_up, ffn_w_down,
              pool_norm, pool_w, pool_scale,
              moe_norm, moe_w_router, moe_w_gate, moe_w_up, moe_w_down,
              final_norm):
    for i in range(DEPTH):
        j = i // 2
        if i % 2 == 0:
            x = x + sliding_window_attention(rms_norm(x, attn_norm[j]), attn_w_qkv[j],
                                             attn_sinks[j], attn_w_o[j])
            x = x + swiglu(rms_norm(x, ffn_norm[j]), ffn_w_gate[j], ffn_w_up[j], ffn_w_down[j])
        else:
            x = x + pooling_mixer(rms_norm(x, pool_norm[j]), pool_w[j], pool_scale[j])
            x = x + moe_swiglu(rms_norm(x, moe_norm[j]), moe_w_router[j],
                               moe_w_gate[j], moe_w_up[j], moe_w_down[j])
    return rms_norm(x, final_norm)


_drawn_inputs = setup_inputs


def setup_inputs(seed=0):
    import zlib

    import numpy as np

    out = dict(_drawn_inputs(seed))
    spreads = {}
    factors = {}
    for name, (base, spread) in spreads.items():
        noise = np.random.default_rng([zlib.crc32(name.encode()), seed]).standard_normal(out[name].shape)
        drawn = base * np.exp(spread * noise) if base else spread * noise
        out[name] = __import__('jax').numpy.asarray(drawn.astype(out[name].dtype))
    for name, factor in factors.items():
        out[name] = (out[name] * factor).astype(out[name].dtype)
    return out
```

```python
from contextlib import ExitStack

import concourse.bass as bass
from concourse import mybir

F32 = mybir.dt.float32
I32 = mybir.dt.int32
U32 = mybir.dt.uint32
ALU = mybir.AluOpType
ACT = mybir.ActivationFunctionType
AX_X = mybir.AxisListType.X

P = 128
BANK = 512
D, S, T = 1024, 256, 2
KD = D // P
HD, NH, NKV = 64, 16, 4
QW, KVW = NH * HD, NKV * HD
F0 = 2816
NE, FE = 8, 3584
EPS = 1e-5
WINDOWS = (2, 4, 8, 16)
FAR = 2.56e32

SLOTS = 4
SLOT = 7168
FFN_TILES = (6, 6, 5, 5)
NFT = sum(FFN_TILES)
FH = FE // 2
FJ = FH // 4
NI = FH // P
ID = NI // 2
BASE, EXT = 64, 32
CAP = BASE + EXT
ROUNDS = -(-S // CAP)
NIT = ROUNDS * NE

C_QKV, C_WO, C_FFN = 0, 3, 5
C_POOL = C_FFN + 12
C_MOE = C_POOL + 1
PER_IT = 12
assert NFT * P == F0 and PER_IT % SLOTS == 0 and ID * D == SLOT and KD * 2 * FJ == SLOT


UNITS = ((0, 0), (0, 1), (1, 0), (1, 1))
HTR_BANK = (0, 1, 4, 5)


def batches_of(u):
    sizes = [2 * (n + 1) for _, n in UNITS]
    first = sum(sizes[:u])
    pairs = [(b, kt) for b in range(2) for kt in ((1,) if UNITS[u][1] == 0 else (0, 1))]
    return [(first + i, b, kt) for i, (b, kt) in enumerate(pairs)]


class Steps:

    def __init__(self, eng, sem):
        self.eng, self.sem, self.n, self.loop = eng, sem, 0, 0

    def step(self, ins):
        ins.then_inc(self.sem, 1)
        self.n += 1

    def wait(self):
        self.eng.wait_ge(self.sem, self.n + self.loop)

    def link(self, ins):
        self.step(ins)
        self.wait()


def trunk_kernel(nc, x, attn_norm, attn_w_qkv, attn_sinks, attn_w_o, ffn_norm, ffn_w_gate, ffn_w_up,
                 ffn_w_down, pool_norm, pool_w, pool_scale, moe_norm, moe_w_router, moe_w_gate,
                 moe_w_up, moe_w_down, final_norm, out):
    with ExitStack() as ctx:
        def sb(name, shape, dt=F32):
            return ctx.enter_context(nc.sbuf_tensor(name, shape, dt))

        def sem(name):
            return ctx.enter_context(nc.semaphore(name))

        bank = [ctx.enter_context(nc.psum_tensor(f"bank{i}", [P, BANK], F32)) for i in range(8)]

        ring = [sb(f"ring{i}", [P, SLOT]) for i in range(SLOTS)]
        xres = sb("xres", [P, T, D])
        nrm = sb("nrm", [P, T, D])
        hT = sb("hT", [P, KD, S])
        arena = sb("arena", [P, 11264])
        ident = sb("ident", [P, P])
        upper = sb("upper", [P, P])
        ones = sb("ones", [P, P])
        gain_rows = sb("gain_rows", [4 * KD, P])
        gains = sb("gains", [P, 4 * KD])
        scale_b = sb("scale_b", [P, D])
        final_b = sb("final_b", [P, D])
        sinks_b = sb("sinks_b", [P, NH])
        router = sb("router", [P, KD, NE])
        dist = sb("dist", [P, 2 * P])
        band = sb("band", [P, 4, S + P])
        iota_i = sb("iota_i", [P, 2 * P], I32)
        iota_f = sb("iota_f", [P, 2 * P])
        slot_id = sb("slot_id", [P, 2 * P])
        eps_t = sb("eps_t", [P, 1])
        warm = sb("warm", [P, 1])
        ssq = sb("ssq", [P, T])
        std = sb("std", [P, T])
        rstd = sb("rstd", [P, T])

        def view(at, *shape):
            n = 1
            for d in shape:
                n *= d
            v = arena[:, at:at + n]
            if len(shape) == 2:
                v = v.rearrange("p (a b) -> p a b", a=shape[0])
            elif len(shape) == 3:
                v = v.rearrange("p (a b c) -> p a b c", a=shape[0], b=shape[1])
            elif len(shape) == 4:
                v = v.rearrange("p (a b c d) -> p a b c d", a=shape[0], b=shape[1], c=shape[2])
            return v

        qT = view(0, 8, S)
        kT = view(2048, 2, S)
        vv = view(2560, T, KVW)
        prob = [view(3072 + 2048 * u, 2, 4, 2 * P) for u in range(2)]
        pT = view(7168, 2, 2, 4, P)
        oT = view(9216, 8, S)
        aT = view(0, NFT, S)
        silu0 = view(5632, 2, S)
        poolT = view(0, KD, S)
        xg = view(0, KD, CAP)
        hid = view(768, FH)
        hidx = view(768 + FH, FH)
        hg = view(768 + 2 * FH, NI, P)
        hgx = view(768 + 3 * FH, NI, BASE)
        at = 768 + 3 * FH + NI * BASE
        sil = view(at, 2, FJ)
        silx = view(at + 2 * FJ, 2, FJ)
        y = view(at + 4 * FJ, BANK)
        yx = view(at + 4 * FJ + BANK, BANK)
        sc = view(at + 4 * FJ + 2 * BANK, 4, P)
        assert at + 4 * FJ + 3 * BANK <= 11264
        disp = sb("disp", [P, T, CAP])
        dispw = sb("dispw", [P, T, 2 * P])

        negm = sb("negm", [P, 2, 8])
        rsum = sb("rsum", [P, 2, 8])
        esink = sb("esink", [P, 2, 8])
        rden = sb("rden", [P, 2, 8])
        lg = sb("lg", [P, T, NE])
        top = sb("top", [P, T, 8])
        topi = sb("topi", [P, T, 8], U32)
        gate2 = sb("gate2", [P, T, 4])
        pick = sb("pick", [P, T, 2, NE])
        mask = sb("mask", [P, T, NE])
        comb = sb("comb", [P, T, NIT + 1])
        slot = sb("slot", [P, T, NIT + 1])
        cnt = sb("cnt", [P, NE])
        flagf = sb("flagf", [P, NIT + 4])
        flags = sb("flags", [P, NIT + 4], I32)
        OVER, LAST = NIT + 2, NIT + 3

        x_in = [sem(f"x_in{t}") for t in range(T)]
        rows_in = sem("rows_in")
        bcast_in = sem("bcast_in")
        full = [sem(f"full{i}") for i in range(SLOTS)]
        pool_step = sem("pool_step")
        dve_step = sem("dve_step")
        act_step = sem("act_step")
        const_ready = sem("const_ready")
        band_counts = sem("band_counts")
        band_ready = sem("band_ready")
        ident_ready = sem("ident_ready")
        dist_ready = sem("dist_ready")
        zeros_ready = sem("zeros_ready")
        pw_scaled = sem("pw_scaled")
        egate_ready = sem("egate_ready")
        disp_part = sem("disp_part")
        gains_T = sem("gains_T")
        gains_ready = sem("gains_ready")
        std_ready = sem("std_ready")
        nrm_ready = sem("nrm_ready")
        x_ready = sem("x_ready")
        tr_done = sem("tr_done")
        hT_ready = sem("hT_ready")
        qkv_done = sem("qkv_done")
        q_ready = sem("q_ready")
        kv_ready = sem("kv_ready")
        s_done = sem("s_done")
        s_read = sem("s_read")
        negm_ready = sem("negm_ready")
        exp_done = sem("exp_done")
        prob_ready = sem("prob_ready")
        pt_done = sem("pt_done")
        pt_ready = sem("pt_ready")
        pv_done = sem("pv_done")
        o_ready = sem("o_ready")
        proj_done = sem("proj_done")
        gu_done = sem("gu_done")
        silu_ready = sem("silu_ready")
        a_ready = sem("a_ready")
        down0_done = sem("down0_done")
        pooled = sem("pooled")
        poolT_ready = sem("poolT_ready")
        mix_done = sem("mix_done")
        logits_done = sem("logits_done")
        mask_ready = sem("mask_ready")
        gap_ready = sem("gap_ready")
        rank_done = sem("rank_done")
        flags_ready = sem("flags_ready")
        disp_ready = sem("disp_ready")
        dispw_ready = sem("dispw_ready")
        gather_done = sem("gather_done")
        xg_ready = sem("xg_ready")
        gate_done = sem("gate_done")
        up_done = sem("up_done")
        gux_done = sem("gux_done")
        sil_ready = sem("sil_ready")
        silx_ready = sem("silx_ready")
        hid_ready = sem("hid_ready")
        hidx_ready = sem("hidx_ready")
        htr_done = sem("htr_done")
        hxtr_done = sem("hxtr_done")
        hgA_ready = sem("hgA_ready")
        hgV_ready = sem("hgV_ready")
        hgxA_ready = sem("hgxA_ready")
        hgxV_ready = sem("hgxV_ready")
        down_done = sem("down_done")
        downx_done = sem("downx_done")
        y_ready = sem("y_ready")
        yx_ready = sem("yx_ready")
        ctr_done = sem("ctr_done")
        sc_ready = sem("sc_ready")
        scat_done = sem("scat_done")
        xadd_done = sem("xadd_done")
        out_ready = sem("out_ready")
        out_sent = sem("out_sent")

        def cols(i, a, w):
            return ring[i][:, 0:a * w].rearrange("p (a w) -> p a w", a=a)

        wqkv = attn_w_qkv[0].rearrange("(k p) n -> p k n", p=P)
        wo = attn_w_o[0].rearrange("(m b i p) n -> m b p i n", m=2, b=2, i=4)
        wg0 = ffn_w_gate[0].rearrange("(k p) n -> p k n", p=P)
        wu0 = ffn_w_up[0].rearrange("(k p) n -> p k n", p=P)
        wd0 = ffn_w_down[0].rearrange("(k p) n -> p k n", p=P)
        pw = pool_w[0].rearrange("g (k p) n -> p (g k) n", p=P)
        stream = []
        for c in (2, 0, 1):
            stream.append([(cols(len(stream) % SLOTS, KD, BANK), wqkv[:, :, c * BANK:(c + 1) * BANK])])
        for m in range(2):
            dst = cols(len(stream) % SLOTS, 4, D)
            stream.append([(dst[64 * b:64 * b + 64], wo[m, b]) for b in range(2)])
        f = 0
        for n in FFN_TILES:
            for w in (wg0, wu0):
                stream.append([(cols(len(stream) % SLOTS, KD, n * P), w[:, :, f * P:(f + n) * P])])
            f += n
        f = 0
        for n in FFN_TILES:
            stream.append([(cols(len(stream) % SLOTS, n, D), wd0[:, f:f + n, :])])
            f += n
        stream.append([(cols(len(stream) % SLOTS, KD, 2 * P), pw)])
        assert len(stream) == C_MOE
        landed = [0] * SLOTS
        ready_at = []
        for n, parts in enumerate(stream):
            landed[n % SLOTS] += 16 * len(parts)
            ready_at.append((n % SLOTS, landed[n % SLOTS]))

        tiles = [sum(FFN_TILES[:j + 1]) for j in range(4)]
        read_by = [(qkv_done, 2), (qkv_done, 4), (qkv_done, 6), (proj_done, 1), (proj_done, 3)]
        read_by += [(gu_done, tiles[j]) for j in range(4) for _ in range(2)]
        read_by += [(down0_done, 1), (down0_done, 2), (down0_done, 3), (down0_done, 5), (mix_done, 2)]
        assert len(read_by) == C_MOE

        def moe_slot(c):
            return (C_MOE + c) % SLOTS

        def moe_full(it, c):
            return landed[moe_slot(c)] + 80 * it + (32, 64, 80)[c // SLOTS]

        block = ctx.enter_context(nc.Block())

        @block.sync
        def _(sp):
            xt = x[0].rearrange("(t p) d -> t p d", p=P)
            sp.dma_start(xres[:, 0, :], xt[0]).then_inc(x_in[0], 16)
            for i, g in enumerate((attn_norm, ffn_norm, pool_norm, moe_norm)):
                sp.dma_start(gain_rows[KD * i:KD * i + KD, :],
                             g[0].rearrange("(k p) -> k p", p=P)).then_inc(rows_in, 16)
            sp.dma_start(xres[:, 1, :], xt[1]).then_inc(x_in[1], 16)
            for n, parts in enumerate(stream):
                if n == 2:
                    for dst, src, w in ((sinks_b, attn_sinks[0:1, :], NH), (scale_b, pool_scale[0:1, :], D),
                                        (final_b, final_norm.rearrange("(a d) -> a d", a=1), D)):
                        sp.dma_start(dst[:, :], src.broadcast_to([P, w])).then_inc(bcast_in, 16)
                    sp.dma_start(router[:, :, :],
                                 moe_w_router[0].rearrange("(k p) e -> p k e", p=P)).then_inc(bcast_in, 16)
                if n >= SLOTS:
                    sp.wait_ge(*read_by[n - SLOTS])
                for dst, src in parts:
                    sp.dma_start(dst, src).then_inc(full[n % SLOTS], 16)

            def load_expert(it, e, first=False):
                for c in range(PER_IT):
                    if c >= SLOTS:
                        b = c - SLOTS
                        sp.wait_ge(up_done if b % 2 else gate_done, 4 * it + b // 2 + 1)
                        sp.wait_ge(gux_done, 4 * it + b // 2 + 1)
                    elif first:
                        sp.wait_ge(*read_by[C_MOE - SLOTS + c])
                    else:
                        sp.wait_ge(down_done, 4 * it + c - 3)
                        sp.wait_ge(downx_done, 4 * it + c - 3)
                    s = moe_slot(c)
                    if c < 8:
                        w = moe_w_up if c % 2 else moe_w_gate
                        w = w[0, bass.ds(e, 1)].rearrange("o (k p) (h j c) -> (o p) k h j c",
                                                          p=P, h=2, j=4)
                        dst = ring[s][:, :].rearrange("p (k h c) -> p k h c", k=KD, h=2)
                        for h in range(2):
                            sp.dma_start(dst[:, :, h, :], w[:, :, h, c // 2, :]).then_inc(full[s], 16)
                    else:
                        w = moe_w_down[0, bass.ds(e, 1)].rearrange("o (c i p) n -> (o p) c i n",
                                                                   p=P, i=ID)
                        sp.dma_start(cols(s, ID, D), w[:, c - 8]).then_inc(full[s], 16)

            load_expert(0, 0, first=True)
            with sp.Fori(1, NE, 1) as it:
                load_expert(it, it)
            sp.wait_ge(flags_ready, 1)
            over = sp.value_load(flags[0:1, OVER:OVER + 1], min_val=0, max_val=1)
            with sp.If(over > 0):
                for r in range(1, ROUNDS):
                    with sp.Fori(0, NE, 1) as e:
                        load_expert(e + r * NE, e)
            with sp.Else():
                pass
            for t in range(T):
                sp.wait_ge(out_ready, t + 1)
                sp.dma_start(out[0].rearrange("(t p) d -> t p d", p=P)[t],
                             hT[:, 4 * t:4 * t + 4, :].rearrange("p k s -> p (k s)")).then_inc(out_sent, 16)
            sp.wait_ge(out_sent, 16 * T)

        @block.gpsimd
        def _(pool):
            own = Steps(pool, pool_step)

            def select(t, pattern, base, mult, op, fill):
                own.link(nc.gpsimd.affine_select(out=t, in_=t, compare_op=op, fill=fill, base=base,
                                                 pattern=pattern, channel_multiplier=mult))

            own.step(nc.gpsimd.memset(eps_t[:, :], EPS))
            own.link(nc.gpsimd.memset(ident[:, :], 0.0))
            nc.gpsimd.affine_select(out=ident[:, :], in_=ident[:, :], compare_op=ALU.not_equal, fill=1.0,
                                    base=0, pattern=[[-1, P]], channel_multiplier=1).then_inc(ident_ready, 1)
            pool.wait_ge(ident_ready, 1)
            own.link(nc.gpsimd.iota(iota_i[:, :], pattern=[[-1, 2 * P]], base=P, channel_multiplier=1))
            own.link(nc.gpsimd.tensor_copy(dist[:, :], iota_i[:, :]))
            select(dist[:, :], [[-1, 2 * P]], P, 1, ALU.is_ge, FAR)
            select(dist[:, :], [[1, 2 * P]], -1, -1, ALU.is_ge, FAR)
            nc.gpsimd.memset(cnt[:, :], 0.0).then_inc(dist_ready, 1)
            own.step(nc.gpsimd.memset(ones[:, :], 1.0))
            own.link(nc.gpsimd.memset(upper[:, :], 1.0))
            select(upper[:, :], [[1, P]], 0, -1, ALU.is_gt, 0.0)
            own.link(nc.gpsimd.iota(iota_i[:, :], pattern=[[1, 2 * P]], base=0, channel_multiplier=0))
            own.link(nc.gpsimd.tensor_copy(iota_f[:, :], iota_i[:, :]))
            for b in range(2):
                own.link(nc.gpsimd.tensor_copy(slot_id[:, BASE * b:BASE * b + BASE], iota_f[:, 0:BASE]))
            for b in range(4):
                own.link(nc.gpsimd.tensor_copy(slot_id[:, P + EXT * b:P + EXT * b + EXT],
                                               iota_f[:, BASE:CAP]))
            nc.gpsimd.memset(flagf[:, :], 0.0).then_inc(const_ready, 1)
            pool.wait_ge(band_counts, 1)
            for g, w in enumerate(WINDOWS):
                b0 = band[:, g, 0:S]
                b1 = band[:, g, S:S + P]
                for b, n in ((b0, S), (b1, P)):
                    select(b, [[1, n]], 0, -1, ALU.is_ge, 0.0)
                    select(b, [[-1, n]], w - 1, 1, ALU.is_ge, 0.0)
                    own.link(nc.gpsimd.tensor_tensor(b[:, 0:P], b[:, 0:P], ident[:, :], ALU.subtract))
            nc.gpsimd.memset(slot[:, :, NIT:NIT + 1], -1.0).then_inc(band_ready, 1)
            pool.wait_ge(x_ready, T)
            own.step(nc.gpsimd.memset(y[:, :], 0.0))
            own.step(nc.gpsimd.memset(yx[:, :], 0.0))
            own.step(nc.gpsimd.memset(comb[:, :, NIT:NIT + 1], 0.0))
            own.wait()
            nc.gpsimd.memset(sc[:, :, :], 0.0).then_inc(zeros_ready, 1)

        @block.scalar
        def _(act):
            own = Steps(act, act_step)
            def preload(func):
                own.wait()
                own.step(nc.scalar.activation(warm[:, :], eps_t[:, :], func))

            act.wait_ge(ident_ready, 1)
            own.step(nc.scalar.activation(warm[:, :], eps_t[:, :], ACT.Sqrt))

            def norm(q, t):
                if q == 0:
                    act.wait_ge(x_in[t], 16)
                else:
                    act.wait_ge(x_ready, T * (q - 1) + t + 1)
                own.link(nc.scalar.activation(nrm[:, t, :], xres[:, t, :], ACT.Square,
                                              accum_out=ssq[:, t:t + 1]))
                nc.scalar.activation(std[:, t:t + 1], ssq[:, t:t + 1], ACT.Sqrt, bias=eps_t[:, 0:1],
                                     scale=1.0 / D).then_inc(std_ready, 1)

            for t in range(T):
                norm(0, t)
            def queries(m):
                for i in (2 * m, 2 * m + 1):
                    act.wait_ge(qkv_done, i + 3)
                    nc.scalar.activation(qT[:, 2 * i:2 * i + 2, :],
                                         bank[4 + i][:, :].rearrange("p (a s) -> p a s", a=2),
                                         ACT.Copy, scale=HD ** -0.5).then_inc(q_ready, 1)

            queries(0)
            preload(ACT.Exp)

            def exps(u, n):
                act.wait_ge(negm_ready, u + 1)
                w0 = P if n == 0 else 0
                for h in range(8):
                    pr = prob[u % 2][:, h // 4, h % 4, w0:]
                    own.step(nc.scalar.activation(pr, pr, ACT.Exp, bias=negm[:, u % 2, h:h + 1],
                                                  accum_out=rsum[:, u % 2, h:h + 1]))
                nc.scalar.activation(esink[:, u % 2, :], esink[:, u % 2, :], ACT.Exp).then_inc(exp_done, 1)

            def keep_pT(u):
                if u >= 1:
                    act.wait_ge(pv_done, u)
                for bt, b, kt in batches_of(u):
                    act.wait_ge(pt_done, bt + 1)
                    nc.scalar.activation(pT[:, b, kt, :, :],
                                         bank[4 + bt % 2][:, :].rearrange("p (i q) -> p i q", i=4),
                                         ACT.Copy).then_inc(pt_ready, 1)

            def keep_o(u, m, n):
                act.wait_ge(pv_done, u + 1)
                nc.scalar.activation(oT[:, 4 * m:4 * m + 4, n * P:n * P + P],
                                     bank[6 + u % 2][:, :].rearrange("p (i q) -> p i q", i=4),
                                     ACT.Copy).then_inc(o_ready, 1)

            for u, (m, n) in enumerate(UNITS):
                if u % 2 == 0:
                    exps(u, UNITS[u][1])
                    exps(u + 1, UNITS[u + 1][1])
                    if u == 0:
                        queries(1)
                keep_pT(u)
                keep_o(u, m, n)

            preload(ACT.Sqrt)
            for t in range(T):
                norm(1, t)
            preload(ACT.Silu)
            for u in range(NFT):
                act.wait_ge(gu_done, u + 1)
                if u >= 2:
                    act.wait_ge(a_ready, u - 1)
                nc.scalar.activation(silu0[:, u % 2, :], bank[u % 4][:, 0:S], ACT.Silu).then_inc(silu_ready, 1)
            preload(ACT.Sqrt)
            for q in (2, 3):
                for t in range(T):
                    norm(q, t)
            preload(ACT.Exp)
            act.wait_ge(gap_ready, 1)
            nc.scalar.activation(gate2[:, :, 1], gate2[:, :, 0], ACT.Exp).then_inc(egate_ready, 1)
            preload(ACT.Silu)
            act.wait_ge(flags_ready, 1)

            def expert(it):
                ext = act.value_load(flags[0:1, bass.ds(it + 1, 1)], min_val=0, max_val=1)
                for j in range(4):
                    act.wait_ge(gate_done, 4 * it + j + 1)
                    if j >= 2:
                        act.wait_ge(hid_ready, 4 * it + j - 1)
                    nc.scalar.activation(sil[:, j % 2, :], bank[2 * (j % 2)][:, 0:FJ],
                                         ACT.Silu).then_inc(sil_ready, 1)
                    with act.If(ext > 0):
                        act.wait_ge(gux_done, 4 * it + j + 1)
                        if j >= 2:
                            act.wait_ge(hidx_ready, 4 * it + j - 1)
                        nc.scalar.activation(silx[0:64, j % 2, :], bank[4 + j % 2][64:128, 0:FJ],
                                             ACT.Silu).then_inc(silx_ready, 1)
                    with act.Else():
                        act.sem_inc(silx_ready, 1)
                for b in (0, 2):
                    act.wait_ge(htr_done, 4 * it + b + 1)
                    i, n = 4 * b, min(4, NI - 4 * b)
                    nc.scalar.activation(hg[:, i:i + n, :],
                                         bank[HTR_BANK[b]][:, 0:n * P].rearrange("p (i s) -> p i s", i=n),
                                         ACT.Copy).then_inc(hgA_ready, 1)
                with act.If(ext > 0):
                    act.wait_ge(hxtr_done, 2 * it + 1)
                    nc.scalar.activation(hgx[:, 0:7, :],
                                         bank[6][:, 0:7 * 64].rearrange("p (i s) -> p i s", i=7),
                                         ACT.Copy).then_inc(hgxA_ready, 1)
                with act.Else():
                    act.sem_inc(hgxA_ready, 1)
                act.wait_ge(down_done, 4 * it + 4)
                nc.scalar.activation(y[:, :], bank[2][:, :], ACT.Copy).then_inc(y_ready, 1)
                act.wait_ge(ctr_done, it + 1)
                nc.scalar.activation(sc[:, :, :], bank[4][:, :].rearrange("p (a q) -> p a q", a=4),
                                     ACT.Copy).then_inc(sc_ready, 1)

            with act.Fori(0, NE, 1) as it:
                expert(it)
            over = act.value_load(flags[0:1, OVER:OVER + 1], min_val=0, max_val=1)
            with act.If(over > 0):
                with act.Fori(NE, NIT, 1) as it:
                    expert(it)
            with act.Else():
                pass
            preload(ACT.Sqrt)
            for t in range(T):
                norm(4, t)

        @block.vector
        def _(dve):
            own = Steps(dve, dve_step)

            def norm(q, t):
                dve.wait_ge(std_ready, T * q + t + 1)
                own.link(nc.vector.reciprocal(rstd[:, t:t + 1], std[:, t:t + 1]))
                if q < 4:
                    nc.vector.tensor_scalar(nrm[:, t, :], xres[:, t, :], rstd[:, t:t + 1], None,
                                            ALU.mult).then_inc(nrm_ready, 1)

            def gained(dst, src, gi, n):
                g = gains[:, gi:gi + n].rearrange("p (k o) -> p k o", o=1)
                return nc.vector.tensor_tensor(dst, src, g.broadcast_to([P, n, dst.shape[2]]), ALU.mult)

            def keep_hT(t, gi, banks, first):
                for kh in range(2):
                    n = 2 * t + kh
                    dve.wait_ge(tr_done, first + n + 1)
                    gained(hT[:, 4 * kh:4 * kh + 4, t * P:t * P + P],
                           bank[banks + n][:, :].rearrange("p (k s) -> p k s", k=4),
                           gi + 4 * kh, 4).then_inc(hT_ready, 1)

            def add_x(t, banks, wait, value):
                dve.wait_ge(wait, value)
                for h in range(2):
                    xs = xres[:, t, h * BANK:h * BANK + BANK]
                    ins = nc.vector.tensor_tensor(xs, bank[banks + 2 * t + h][:, :], xs, ALU.add)
                    if h == 0:
                        own.step(ins)
                    else:
                        own.wait()
                        ins.then_inc(x_ready, 1)

            norm(0, 0)
            norm(0, 1)
            dve.wait_ge(gains_T, 1)
            nc.vector.tensor_copy(gains[:, :], bank[7][:, 0:4 * KD]).then_inc(gains_ready, 1)
            dve.wait_ge(gains_ready, 1)
            for t in range(T):
                keep_hT(t, 0, 0, 0)
            dve.wait_ge(qkv_done, 1)
            nc.vector.tensor_copy(kT[:, :, :], bank[0][:, :].rearrange("p (m s) -> p m s", m=2)).then_inc(kv_ready, 1)
            dve.wait_ge(qkv_done, 2)
            nc.vector.tensor_copy(vv[:, :, :], bank[1][:, :].rearrange("p (t c) -> p t c", t=2)).then_inc(kv_ready, 1)
            dve.wait_ge(bcast_in, 64)
            dve.wait_ge(const_ready, 1)
            for g, w in enumerate(WINDOWS):
                own.step(nc.vector.tensor_scalar(band[:, g, 0:S], iota_f[:, :], 1.0, float(w),
                                                 ALU.add, ALU.min))
                own.step(nc.vector.memset(band[:, g, S:S + P], 1.0 / w))
            own.wait()
            nc.vector.reciprocal(band[:, :, 0:S], band[:, :, 0:S]).then_inc(band_counts, 1)
            dve.wait_ge(dist_ready, 1)

            def scores(u, m, n):
                w0 = P if n == 0 else 0
                pr = prob[u % 2]
                dve.wait_ge(s_done, u + 1)
                if u >= 2:
                    dve.wait_ge(pt_done, batches_of(u - 2)[-1][0] + 1)
                for h in range(8):
                    slope = 2.0 ** (-8.0 * (8 * m + h + 1) / NH)
                    ins = nc.vector.scalar_tensor_tensor(
                        out=pr[:, h // 4, h % 4, w0:], in0=dist[:, w0:], scalar=-slope,
                        in1=bank[h // 2][:, (h % 2) * 2 * P + w0:(h % 2 + 1) * 2 * P],
                        op0=ALU.mult, op1=ALU.add)
                    if h < 7:
                        own.step(ins)
                    else:
                        ins.then_inc(s_read, 1)
                own.wait()
                dve.wait_ge(s_read, u + 1)
                nm, es, sk = negm[:, u % 2, :], esink[:, u % 2, :], sinks_b[:, 8 * m:8 * m + 8]
                own.link(nc.vector.reduce_max(nm, pr[:, :, :, w0:].rearrange("p b i k -> p (b i) k"), axis=AX_X))
                own.link(nc.vector.tensor_tensor(nm, nm, sk, ALU.max))
                own.link(nc.vector.tensor_scalar(nm, nm, -1.0, None, ALU.mult))
                nc.vector.tensor_tensor(es, sk, nm, ALU.add).then_inc(negm_ready, 1)

            def normalise(u, n):
                w0 = P if n == 0 else 0
                dve.wait_ge(exp_done, u + 1)
                rd = rden[:, u % 2, :]
                own.link(nc.vector.tensor_tensor(rd, rsum[:, u % 2, :], esink[:, u % 2, :], ALU.add))
                own.link(nc.vector.reciprocal(rd, rd))
                pr = prob[u % 2][:, :, :, w0:].rearrange("p b i k -> p (b i) k")
                r = rd.rearrange("p (h o) -> p h o", o=1).broadcast_to([P, 8, 2 * P - w0])
                nc.vector.tensor_tensor(pr, pr, r, ALU.mult).then_inc(prob_ready, 1)

            for u in (0, 2):
                scores(u, *UNITS[u])
                scores(u + 1, *UNITS[u + 1])
                normalise(u, UNITS[u][1])
                normalise(u + 1, UNITS[u + 1][1])
            for t in range(T):
                add_x(t, 0, proj_done, t + 2)
                norm(1, t)
            for t in range(T):
                keep_hT(t, KD, 4, 2 * T)
            for u in range(NFT):
                dve.wait_ge(silu_ready, u + 1)
                nc.vector.tensor_tensor(aT[:, u, :], bank[u % 4][:, S:2 * S], silu0[:, u % 2, :],
                                        ALU.mult).then_inc(a_ready, 1)
            dve.wait_ge(full[ready_at[C_POOL][0]], ready_at[C_POOL][1])
            maps = stream[C_POOL][0][0].rearrange("p (g k) c -> p g k c", k=2)
            for k in range(2):
                own.step(nc.vector.tensor_tensor(maps[:, :, k, :], maps[:, :, k, :],
                                                 scale_b[:, :].rearrange("p (g c) -> p g c", g=4), ALU.mult))
            own.wait()
            dve.sem_inc(pw_scaled, 1)
            for t in range(T):
                add_x(t, 4, down0_done, t + 4)
                norm(2, t)
            for g in range(4):
                dve.wait_ge(pooled, g + 1)
                gained(poolT[:, 2 * g:2 * g + 2, :], bank[g][:, :].rearrange("p (k s) -> p k s", k=2),
                       2 * KD + 2 * g, 2).then_inc(poolT_ready, 1)
            for t in range(T):
                add_x(t, 4, mix_done, t + 1)
                norm(3, t)
            for t in range(T):
                keep_hT(t, 3 * KD, 0, 4 * T)

            dve.wait_ge(logits_done, 1)
            dve.wait_ge(band_ready, 1)
            own.link(nc.vector.tensor_copy(lg[:, :, :], bank[4][:, 0:T * NE].rearrange("p (t e) -> p t e", t=T)))
            for t in range(T):
                own.link(nc.vector.max(top[:, t, :], lg[:, t, :]))
                own.link(nc.vector.max_index(topi[:, t, :], top[:, t, :], lg[:, t, :]))
            cols8 = iota_f[:, 0:NE].rearrange("p (t e) -> p t e", t=1).broadcast_to([P, T, NE])
            for j in range(2):
                own.step(nc.vector.tensor_tensor(pick[:, :, j, :], cols8,
                                                 topi[:, :, j:j + 1].broadcast_to([P, T, NE]), ALU.is_equal))
            own.wait()
            nc.vector.tensor_tensor(mask[:, :, :], pick[:, :, 0, :], pick[:, :, 1, :],
                                    ALU.add).then_inc(mask_ready, 1)
            nc.vector.tensor_tensor(gate2[:, :, 0], top[:, :, 1], top[:, :, 0],
                                    ALU.subtract).then_inc(gap_ready, 1)
            dve.wait_ge(mask_ready, 1)
            dve.wait_ge(rank_done, 1)
            own.link(nc.vector.scalar_tensor_tensor(
                out=slot[:, :, 0:NE], in0=bank[5][:, 0:T * NE].rearrange("p (t e) -> p t e", t=T),
                scalar=1000.0, in1=mask[:, :, :], op0=ALU.add, op1=ALU.mult))
            own.link(nc.vector.tensor_scalar(slot[:, :, 0:NE], slot[:, :, 0:NE], -1000.0, None, ALU.add))
            def dispatch(it):
                for t in range(T):
                    ins = nc.vector.tensor_scalar(disp[:, t, :], iota_f[:, 0:CAP],
                                                  slot[:, t, bass.ds(it, 1)], None, ALU.is_equal)
                    if t == 0:
                        ins.then_inc(disp_part, 1)
                    else:
                        ins.then_inc(disp_ready, 1)

            def keep_xg(n):
                dve.wait_ge(gather_done, n)
                for h in range(2):
                    ins = gained(xg[:, 4 * h:4 * h + 4, :],
                                 bank[6 + h][:, 0:4 * CAP].rearrange("p (k s) -> p k s", k=4),
                                 3 * KD + 4 * h, 4)
                    ins.then_inc(xg_ready, 1)

            def scattered(n, t):
                dve.wait_ge(scat_done, n * T + t + 1)
                for h in range(2):
                    hs = slice(h * BANK, h * BANK + BANK)
                    nc.vector.tensor_tensor(xres[:, t, hs], bank[6 + h][:, :], xres[:, t, hs],
                                            ALU.add).then_inc(xadd_done, 1)

            dispatch(0)
            dve.wait_ge(egate_ready, 1)
            own.link(nc.vector.tensor_scalar(gate2[:, :, 2], gate2[:, :, 1], 1.0, None, ALU.add))
            own.link(nc.vector.reciprocal(gate2[:, :, 2], gate2[:, :, 2]))
            own.link(nc.vector.tensor_tensor(gate2[:, :, 3], gate2[:, :, 1], gate2[:, :, 2], ALU.mult))
            for t in range(T):
                own.link(nc.vector.tensor_scalar(comb[:, t, 0:NE], pick[:, t, 0, :], gate2[:, t, 2:3],
                                                 None, ALU.mult))
                own.link(nc.vector.scalar_tensor_tensor(
                    out=comb[:, t, 0:NE], in0=pick[:, t, 1, :], scalar=gate2[:, t, 3:4],
                    in1=comb[:, t, 0:NE], op0=ALU.mult, op1=ALU.add))
            for r in range(1, ROUNDS):
                own.step(nc.vector.tensor_copy(comb[:, :, r * NE:r * NE + NE], comb[:, :, 0:NE]))
                own.step(nc.vector.tensor_scalar(slot[:, :, r * NE:r * NE + NE], slot[:, :, 0:NE],
                                                 float(CAP * r), None, ALU.subtract))
            own.link(nc.vector.tensor_copy(cnt[:, :], bank[5][:, T * NE:T * NE + NE]))
            for r in range(ROUNDS):
                own.step(nc.vector.tensor_scalar(flagf[:, 1 + r * NE:1 + r * NE + NE], cnt[:, :],
                                                 float(CAP * r + BASE), None, ALU.is_gt))
            own.link(nc.vector.reduce_max(flagf[:, OVER:OVER + 1], cnt[:, :], axis=AX_X))
            own.link(nc.vector.tensor_scalar(flagf[:, OVER:OVER + 1], flagf[:, OVER:OVER + 1],
                                             float(CAP), None, ALU.is_gt))
            nc.vector.tensor_copy(flags[:, :], flagf[:, :]).then_inc(flags_ready, 1)
            keep_xg(1)
            dve.wait_ge(flags_ready, 1)
            dve.wait_ge(zeros_ready, 1)

            def expert(it):
                ext = dve.value_load(flags[0:1, bass.ds(it + 1, 1)], min_val=0, max_val=1)
                dve.wait_ge(ctr_done, it)
                for t in range(T):
                    nc.vector.tensor_scalar(dispw[:, t, :], slot_id[:, :], slot[:, t, bass.ds(it, 1)],
                                            comb[:, t, bass.ds(it, 1)], ALU.is_equal,
                                            ALU.mult).then_inc(dispw_ready, 1)
                dve.wait_ge(xadd_done, 4 * it)
                for j in range(4):
                    js = slice(j * FJ, j * FJ + FJ)
                    dve.wait_ge(up_done, 4 * it + j + 1)
                    dve.wait_ge(sil_ready, 4 * it + j + 1)
                    nc.vector.tensor_tensor(hid[:, js], bank[2 * (j % 2) + 1][:, 0:FJ], sil[:, j % 2, :],
                                            ALU.mult).then_inc(hid_ready, 1)
                    with dve.If(ext > 0):
                        dve.wait_ge(silx_ready, 4 * it + j + 1)
                        nc.vector.tensor_tensor(hidx[0:64, js], bank[4 + j % 2][0:64, 0:FJ],
                                                silx[0:64, j % 2, :], ALU.mult).then_inc(hidx_ready, 1)
                    with dve.Else():
                        dve.sem_inc(hidx_ready, 1)
                    if j < 2:
                        scattered(it, j)
                    if j == 1:
                        dve.wait_ge(gather_done, it + 1)
                        dispatch(it + 1)
                keep_xg(it + 2)
                for b in (1, 3):
                    i, n = 4 * b, min(4, NI - 4 * b)
                    dve.wait_ge(htr_done, 4 * it + b + 1)
                    nc.vector.tensor_copy(hg[:, i:i + n, :],
                                          bank[HTR_BANK[b]][:, 0:n * P].rearrange("p (i s) -> p i s", i=n)
                                          ).then_inc(hgV_ready, 1)
                with dve.If(ext > 0):
                    dve.wait_ge(hxtr_done, 2 * it + 2)
                    nc.vector.tensor_copy(hgx[:, 7:14, :],
                                          bank[7][:, 0:7 * 64].rearrange("p (i s) -> p i s", i=7)
                                          ).then_inc(hgxV_ready, 1)
                    dve.wait_ge(downx_done, 4 * it + 4)
                    nc.vector.tensor_copy(yx[:, :], bank[3][:, :]).then_inc(yx_ready, 1)
                with dve.Else():
                    dve.sem_inc(hgxV_ready, 1)
                    dve.sem_inc(yx_ready, 1)

            def final(n):
                dve.wait_ge(xadd_done, 4 * n)
                for t in range(T):
                    scattered(n, t)
                    dve.wait_ge(xadd_done, 4 * n + 2 * t + 2)
                    dve.sem_inc(x_ready, 1)

            with dve.Fori(0, NE, 1) as it:
                expert(it)
            over = dve.value_load(flags[0:1, OVER:OVER + 1], min_val=0, max_val=1)
            with dve.If(over > 0):
                with dve.Fori(NE, NIT, 1) as it:
                    expert(it)
                final(NIT)
            with dve.Else():
                final(NE)
            for t in range(T):
                norm(4, t)
                nc.vector.scalar_tensor_tensor(
                    out=hT[:, 4 * t:4 * t + 4, :].rearrange("p k s -> p (k s)"), in0=xres[:, t, :],
                    scalar=rstd[:, t:t + 1], in1=final_b[:, :], op0=ALU.mult,
                    op1=ALU.mult).then_inc(out_ready, 1)

        @block.tensor
        def _(pe):
            mm = nc.tensor.matmul

            def chunk_landed(n):
                pe.wait_ge(full[ready_at[n][0]], ready_at[n][1])

            def transposes(q, banks):
                for t in range(T):
                    pe.wait_ge(nrm_ready, T * q + t + 1)
                    for kh in range(2):
                        for k in range(4):
                            c = (4 * kh + k) * P
                            last = nc.tensor.transpose(bank[banks + 2 * t + kh][:, k * P:k * P + P],
                                                       nrm[:, t, c:c + P], ident[:, :])
                        last.then_inc(tr_done, 1)

            pe.wait_ge(ident_ready, 1)
            pe.wait_ge(rows_in, 64)
            nc.tensor.transpose(bank[7][:, 0:4 * KD], gain_rows[:, :],
                                ident[0:4 * KD, 0:4 * KD]).then_inc(gains_T, 1)
            transposes(0, 0)
            pe.wait_ge(hT_ready, 2 * T)
            pe.wait_ge(gains_ready, 1)
            chunk_landed(C_QKV)
            w = stream[C_QKV][0][0]
            for m in range(2):
                for k in range(KD):
                    last = mm(bank[0][:, m * S:m * S + S], w[:, k, m * P:m * P + P], hT[:, k, :],
                              start=k == 0, stop=k == KD - 1)
            last.then_inc(qkv_done, 1)
            for t in range(T):
                for k in range(KD):
                    last = mm(bank[1][:, t * KVW:t * KVW + KVW], hT[:, k, t * P:t * P + P],
                              w[:, k, KVW:2 * KVW], start=k == 0, stop=k == KD - 1)
            last.then_inc(qkv_done, 1)

            def queries(m):
                chunk_landed(C_QKV + 1 + m)
                w = stream[C_QKV + 1 + m][0][0]
                for i in range(4):
                    for k in range(KD):
                        for b in range(2):
                            c = (4 * b + i) * HD
                            last = mm(bank[4 + 2 * m + i // 2][64 * b:64 * b + 64, (i % 2) * S:(i % 2) * S + S],
                                      w[:, k, c:c + HD], hT[:, k, :], start=k == 0, stop=k == KD - 1)
                    if i % 2:
                        last.then_inc(qkv_done, 1)

            def scores(u, m, n):
                pe.wait_ge(q_ready, 2 * m + 2)
                if u == 0:
                    pe.wait_ge(kv_ready, 2)
                else:
                    pe.wait_ge(s_read, u)
                w0 = P if n == 0 else 0
                for i in range(4):
                    for b in range(2):
                        last = mm(bank[2 * b + i // 2][:, (i % 2) * 2 * P + w0:(i % 2 + 1) * 2 * P],
                                  qT[64 * b:64 * b + 64, 4 * m + i, n * P:n * P + P],
                                  kT[64 * b:64 * b + 64, m, 0:2 * P - w0], start=True, stop=True)
                last.then_inc(s_done, 1)

            def values(u, m, n):
                pe.wait_ge(prob_ready, u + 1)
                for bt, b, kt in batches_of(u):
                    if bt >= 2:
                        pe.wait_ge(pt_ready, bt - 1)
                    else:
                        pe.wait_ge(q_ready, 2)
                    for i in range(4):
                        last = nc.tensor.transpose(bank[4 + bt % 2][:, i * P:i * P + P],
                                                   prob[u % 2][:, b, i, kt * P:kt * P + P], ident[:, :])
                    last.then_inc(pt_done, 1)
                if u < 2:
                    pe.wait_ge(q_ready, 4)
                else:
                    pe.wait_ge(o_ready, u - 1)
                pe.wait_ge(pt_ready, batches_of(u)[-1][0] + 1)
                kts = (1,) if n == 0 else (0, 1)
                for kt in kts:
                    for b in range(2):
                        g = 2 * m + b
                        last = mm(bank[6 + u % 2][64 * b:64 * b + 64, :],
                                  vv[:, n - 1 + kt, g * HD:g * HD + HD],
                                  pT[:, b, kt, :, :].rearrange("p i q -> p (i q)"),
                                  start=kt == kts[0], stop=kt == 1)
                last.then_inc(pv_done, 1)

            def project(m):
                pe.wait_ge(o_ready, 2 * m + 2)
                chunk_landed(C_WO + m)
                w = cols((C_WO + m) % SLOTS, 4, D)
                for t in range(T):
                    for i in range(4):
                        for h in range(2):
                            last = mm(bank[2 * t + h][:, :], oT[:, 4 * m + i, t * P:t * P + P],
                                      w[:, i, h * BANK:h * BANK + BANK], start=m == 0 and i == 0,
                                      stop=m == 1 and i == 3)
                    if m == 1 or t == 1:
                        last.then_inc(proj_done, 1)

            queries(0)
            scores(0, *UNITS[0])
            scores(1, *UNITS[1])
            queries(1)
            values(0, *UNITS[0])
            scores(2, *UNITS[2])
            values(1, *UNITS[1])
            scores(3, *UNITS[3])
            pe.wait_ge(s_read, 4)
            project(0)
            values(2, *UNITS[2])
            values(3, *UNITS[3])
            project(1)

            transposes(1, 4)
            pe.wait_ge(hT_ready, 4 * T)
            u = 0
            for j, n in enumerate(FFN_TILES):
                c = C_FFN + 2 * j
                chunk_landed(c)
                chunk_landed(c + 1)
                for f in range(n):
                    if u >= 4:
                        pe.wait_ge(a_ready, u - 3)
                    for half, w in enumerate((stream[c][0][0], stream[c + 1][0][0])):
                        for k in range(KD):
                            last = mm(bank[u % 4][:, half * S:half * S + S], w[:, k, f * P:f * P + P],
                                      hT[:, k, :], start=k == 0, stop=k == KD - 1)
                    last.then_inc(gu_done, 1)
                    u += 1
            pe.wait_ge(a_ready, NFT)
            u = 0
            for j, n in enumerate(FFN_TILES):
                c = C_FFN + 8 + j
                chunk_landed(c)
                w = stream[c][0][0]
                order = [(t, f) for f in range(n) for t in range(T)]
                if j == 3:
                    order.sort()
                for t, f in order:
                    for h in range(2):
                        last = mm(bank[4 + 2 * t + h][:, :], aT[:, u + f, t * P:t * P + P],
                                  w[:, f, h * BANK:h * BANK + BANK], start=u + f == 0, stop=u + f == NFT - 1)
                    if j == 3 and f == n - 1 and t == 0:
                        last.then_inc(down0_done, 1)
                last.then_inc(down0_done, 1)
                u += n

            pe.wait_ge(nrm_ready, 3 * T)
            pe.wait_ge(band_ready, 1)
            for g in range(4):
                for k in range(2):
                    c = (2 * g + k) * P
                    mm(bank[g][:, k * S:k * S + S], nrm[:, 0, c:c + P], band[:, g, 0:S],
                       start=True, stop=False)
                    last = mm(bank[g][:, k * S + P:k * S + S], nrm[:, 1, c:c + P], band[:, g, S:S + P],
                              start=False, stop=True)
                last.then_inc(pooled, 1)
            pe.wait_ge(poolT_ready, 4)
            pe.wait_ge(pw_scaled, 1)
            w = stream[C_POOL][0][0]
            for t in range(T):
                for g in range(4):
                    for k in range(2):
                        last = mm(bank[4 + 2 * t + g // 2][:, (g % 2) * 2 * P:(g % 2 + 1) * 2 * P],
                                  poolT[:, 2 * g + k, t * P:t * P + P], w[:, 2 * g + k, :],
                                  start=k == 0, stop=k == 1)
                last.then_inc(mix_done, 1)

            transposes(3, 0)
            pe.wait_ge(bcast_in, 64)
            pe.wait_ge(const_ready, 1)
            for t in range(T):
                pe.wait_ge(hT_ready, 4 * T + 2 * t + 2)
                for k in range(KD):
                    last = mm(bank[4][:, t * NE:t * NE + NE], hT[:, k, t * P:t * P + P], router[:, k, :],
                              start=k == 0, stop=k == KD - 1)
            last.then_inc(logits_done, 1)
            pe.wait_ge(mask_ready, 1)
            mm(bank[5][:, 0:NE], upper[:, :], mask[:, 0, :], start=True, stop=True)
            mm(bank[5][:, NE:2 * NE], ones[:, :], mask[:, 0, :], start=True, stop=False)
            mm(bank[5][:, NE:2 * NE], upper[:, :], mask[:, 1, :], start=False, stop=True)
            mm(bank[5][:, 2 * NE:3 * NE], ones[:, :], mask[:, 0, :], start=True, stop=False)
            mm(bank[5][:, 2 * NE:3 * NE], ones[:, :], mask[:, 1, :], start=False, stop=True).then_inc(rank_done, 1)

            def gather(n):
                pe.wait_ge(disp_ready, n)
                pe.wait_ge(disp_part, n)
                for k in range(KD):
                    for t in range(T):
                        last = mm(bank[6 + k // 4][:, (k % 4) * CAP:(k % 4) * CAP + CAP],
                                  nrm[:, t, k * P:k * P + P], disp[:, t, :], start=t == 0, stop=t == 1)
                last.then_inc(gather_done, 1)

            def scatter(ext, n, t):
                with pe.If(ext > 0):
                    for h in range(2):
                        hp = slice(64 * h, 64 * h + 64)
                        mm(bank[6 + h][:, :], sc[hp, t, :], y[hp, :], start=True, stop=False)
                    for h in range(2):
                        hp = slice(64 * h, 64 * h + 64)
                        last = mm(bank[6 + h][:, :], sc[hp, T + t, :], yx[hp, :], start=False, stop=True)
                    last.then_inc(scat_done, 1)
                with pe.Else():
                    for h in range(2):
                        hp = slice(64 * h, 64 * h + 64)
                        last = mm(bank[6 + h][:, :], sc[hp, t, :], y[hp, :], start=True, stop=True)
                    last.then_inc(scat_done, 1)

            def gate_up(it, j, ext):
                for up in range(2):
                    c = 2 * j + up
                    pe.wait_ge(full[moe_slot(c)], moe_full(it, c))
                    if j >= 2:
                        pe.wait_ge(hid_ready if up else sil_ready, 4 * it + j - 1)
                    elif j == 1:
                        pe.wait_ge(yx_ready if up else y_ready, it)
                    w = ring[moe_slot(c)][:, :].rearrange("p (k h c) -> p k h c", k=KD, h=2)
                    for k in range(KD):
                        for h in range(2):
                            last = mm(bank[2 * (j % 2) + up][64 * h:64 * h + 64, 0:FJ], xg[:, k, 0:BASE],
                                      w[:, k, h, :], start=k == 0, stop=k == KD - 1)
                    last.then_inc(up_done if up else gate_done, 1)
                with pe.If(ext > 0):
                    if j >= 2:
                        pe.wait_ge(hidx_ready, 4 * it + j - 1)
                    elif j == 0:
                        pe.wait_ge(sc_ready, it)
                    ws = [ring[moe_slot(2 * j + g)][:, :].rearrange("p (k h c) -> p k h c", k=KD, h=2)
                          for g in range(2)]
                    for k in range(KD):
                        for q in range(4):
                            last = mm(bank[4 + j % 2][32 * q:32 * q + 32, 0:FJ], xg[:, k, BASE:CAP],
                                      ws[1 - q // 2][:, k, q % 2, :], start=k == 0, stop=k == KD - 1)
                    last.then_inc(gux_done, 1)
                with pe.Else():
                    pe.sem_inc(gux_done, 1)

            def expert(it):
                extp = pe.value_load(flags[0:1, bass.ds(it, 1)], min_val=0, max_val=1)
                ext = pe.value_load(flags[0:1, bass.ds(it + 1, 1)], min_val=0, max_val=1)
                pe.wait_ge(xg_ready, 2 * it + 2)
                gate_up(it, 0, ext)
                pe.wait_ge(y_ready, it)
                pe.wait_ge(yx_ready, it)
                pe.wait_ge(sc_ready, it)
                scatter(extp, it, 0)
                gate_up(it, 1, ext)
                pe.wait_ge(xadd_done, 4 * it + 2)
                scatter(extp, it, 1)
                gate_up(it, 2, ext)
                gate_up(it, 3, ext)
                pe.wait_ge(xadd_done, 4 * it + 4)
                gather(it + 2)
                for b in range(4):
                    pe.wait_ge(hid_ready, 4 * it + min(b + 3, 4) if b < 2 else 4 * it + 4)
                    if b >= 2:
                        pe.wait_ge(hidx_ready, 4 * it + b + 1)
                    for i in range(4 * b, min(4 * b + 4, NI)):
                        last = nc.tensor.transpose(bank[HTR_BANK[b]][:, (i % 4) * P:(i % 4) * P + P],
                                                   hid[:, i * P:i * P + P], ident[:, :])
                    last.then_inc(htr_done, 1)
                pe.wait_ge(xg_ready, 2 * it + 4)
                with pe.If(ext > 0):
                    for b in range(2):
                        for i in range(7):
                            c = (7 * b + i) * P
                            last = nc.tensor.transpose(bank[6 + b][:, i * 64:i * 64 + 64],
                                                       hidx[0:64, c:c + P], ident[0:64, 0:64])
                        last.then_inc(hxtr_done, 1)
                with pe.Else():
                    pe.sem_inc(hxtr_done, 2)
                pe.wait_ge(hgA_ready, 2 * it + 2)
                pe.wait_ge(hgV_ready, 2 * it + 2)
                for d in range(4):
                    c = 8 + d
                    pe.wait_ge(full[moe_slot(c)], moe_full(it, c))
                    w = cols(moe_slot(c), ID, D)
                    half, i0 = d // 2, (d % 2) * ID
                    for i in range(ID):
                        for h in range(2):
                            last = mm(bank[2][64 * h:64 * h + 64, :],
                                      hg[:, i0 + i, half * BASE:half * BASE + BASE],
                                      w[:, i, h * BANK:h * BANK + BANK],
                                      start=d == 0 and i == 0, stop=d == 3 and i == ID - 1)
                    last.then_inc(down_done, 1)
                    with pe.If(ext > 0):
                        pe.wait_ge(hgxA_ready, it + 1)
                        pe.wait_ge(hgxV_ready, it + 1)
                        for i in range(ID):
                            ii = i0 + i
                            for h in range(2):
                                q = 64 * h + 32 * (ii % 2)
                                last = mm(bank[3][q:q + 32, :], hgx[:, ii, half * EXT:half * EXT + EXT],
                                          w[:, i, h * BANK:h * BANK + BANK],
                                          start=half == 0 and ii < 2, stop=half == 1 and ii >= NI - 2)
                        last.then_inc(downx_done, 1)
                    with pe.Else():
                        pe.sem_inc(downx_done, 1)
                pe.wait_ge(dispw_ready, 2 * it + 2)
                for a in range(2):
                    for t in range(T):
                        last = nc.tensor.transpose(bank[4][:, (2 * a + t) * P:(2 * a + t + 1) * P],
                                                   dispw[:, t, a * P:a * P + P], ident[:, :])
                last.then_inc(ctr_done, 1)

            def final(n):
                ext = pe.value_load(flags[0:1, n:n + 1], min_val=0, max_val=1)
                pe.wait_ge(y_ready, n)
                pe.wait_ge(yx_ready, n)
                pe.wait_ge(sc_ready, n)
                pe.wait_ge(xg_ready, 2 * n + 2)
                scatter(ext, n, 0)
                pe.wait_ge(xadd_done, 4 * n + 2)
                scatter(ext, n, 1)

            gather(1)
            pe.wait_ge(flags_ready, 1)
            pe.wait_ge(zeros_ready, 1)
            with pe.Fori(0, NE, 1) as it:
                expert(it)
            over = pe.value_load(flags[0:1, OVER:OVER + 1], min_val=0, max_val=1)
            with pe.If(over > 0):
                with pe.Fori(NE, NIT, 1) as it:
                    expert(it)
                final(NIT)
            with pe.Else():
                final(NE)


_INS = ["x", "attn_norm", "attn_w_qkv", "attn_sinks", "attn_w_o", "ffn_norm", "ffn_w_gate", "ffn_w_up",
        "ffn_w_down", "pool_norm", "pool_w", "pool_scale", "moe_norm", "moe_w_router", "moe_w_gate",
        "moe_w_up", "moe_w_down", "final_norm"]


def kernel(**inputs):
    import numpy as np
    import concourse.bacc as bacc
    from concourse.bass_utils import run_bass_kernel_spmd

    nc = bacc.Bacc("TRN2", target_bir_lowering=False, num_devices=1)
    arrays, args = {}, []
    for name in _INS:
        a = np.ascontiguousarray(inputs[name])
        arrays[name] = a
        args.append(nc.dram_tensor(name, a.shape, mybir.dt.from_np(a.dtype), kind="ExternalInput").ap())
    args.append(nc.dram_tensor("out", (1, S, D), F32, kind="ExternalOutput").ap())
    trunk_kernel(nc, *args)
    r = run_bass_kernel_spmd(nc, [arrays], core_ids=[0])
    return r.results[0]["out"]
```

```python
from contextlib import ExitStack

import concourse.bass as bass
from concourse import mybir

F32 = mybir.dt.float32
I32 = mybir.dt.int32
U32 = mybir.dt.uint32
ALU = mybir.AluOpType
ACT = mybir.ActivationFunctionType
AX_X = mybir.AxisListType.X

P = 128
BANK = 512
D, S, T = 1024, 256, 2
KD = D // P
HD, NH, NKV = 64, 16, 4
QW, KVW = NH * HD, NKV * HD
F0 = 2816
NE, FE = 8, 3584
EPS = 1e-5
WINDOWS = (2, 4, 8, 16)
FAR = 2.56e32

SLOTS = 4
SLOT = 7168
FFN_TILES = (6, 6, 5, 5)
NFT = sum(FFN_TILES)
FH = FE // 2
FJ = FH // 4
NI = FH // P
ID = NI // 2
BASE, EXT = 64, 32
CAP = BASE + EXT
ROUNDS = -(-S // CAP)
NIT = ROUNDS * NE

C_QKV, C_WO, C_FFN = 0, 3, 5
C_POOL = C_FFN + 12
C_MOE = C_POOL + 1
PER_IT = 12
assert NFT * P == F0 and PER_IT % SLOTS == 0 and ID * D == SLOT and KD * 2 * FJ == SLOT


UNITS = ((0, 0), (0, 1), (1, 0), (1, 1))
HTR_BANK = (0, 1, 4, 5)


def batches_of(u):
    sizes = [2 * (n + 1) for _, n in UNITS]
    first = sum(sizes[:u])
    pairs = [(b, kt) for b in range(2) for kt in ((1,) if UNITS[u][1] == 0 else (0, 1))]
    return [(first + i, b, kt) for i, (b, kt) in enumerate(pairs)]


class Steps:

    def __init__(self, eng, sem):
        self.eng, self.sem, self.n, self.loop = eng, sem, 0, 0

    def step(self, ins):
        ins.then_inc(self.sem, 1)
        self.n += 1

    def wait(self):
        self.eng.wait_ge(self.sem, self.n + self.loop)

    def link(self, ins):
        self.step(ins)
        self.wait()


def trunk_kernel(nc, x, attn_norm, attn_w_qkv, attn_sinks, attn_w_o, ffn_norm, ffn_w_gate, ffn_w_up,
                 ffn_w_down, pool_norm, pool_w, pool_scale, moe_norm, moe_w_router, moe_w_gate,
                 moe_w_up, moe_w_down, final_norm, out):
    with ExitStack() as ctx:
        def sb(name, shape, dt=F32):
            return ctx.enter_context(nc.sbuf_tensor(name, shape, dt))

        def sem(name):
            return ctx.enter_context(nc.semaphore(name))

        bank = [ctx.enter_context(nc.psum_tensor(f"bank{i}", [P, BANK], F32)) for i in range(8)]

        ring = [sb(f"ring{i}", [P, SLOT]) for i in range(SLOTS)]
        xres = sb("xres", [P, T, D])
        nrm = sb("nrm", [P, T, D])
        hT = sb("hT", [P, KD, S])
        arena = sb("arena", [P, 11264])
        ident = sb("ident", [P, P])
        upper = sb("upper", [P, P])
        ones = sb("ones", [P, P])
        gain_rows = sb("gain_rows", [4 * KD, P])
        gains = sb("gains", [P, 4 * KD])
        scale_b = sb("scale_b", [P, D])
        final_b = sb("final_b", [P, D])
        sinks_b = sb("sinks_b", [P, NH])
        router = sb("router", [P, KD, NE])
        dist = sb("dist", [P, 2 * P])
        band = sb("band", [P, 4, S + P])
        iota_i = sb("iota_i", [P, 2 * P], I32)
        iota_f = sb("iota_f", [P, 2 * P])
        slot_id = sb("slot_id", [P, 2 * P])
        eps_t = sb("eps_t", [P, 1])
        warm = sb("warm", [P, 1])
        ssq = sb("ssq", [P, T])
        std = sb("std", [P, T])
        rstd = sb("rstd", [P, T])

        def view(at, *shape):
            n = 1
            for d in shape:
                n *= d
            v = arena[:, at:at + n]
            if len(shape) == 2:
                v = v.rearrange("p (a b) -> p a b", a=shape[0])
            elif len(shape) == 3:
                v = v.rearrange("p (a b c) -> p a b c", a=shape[0], b=shape[1])
            elif len(shape) == 4:
                v = v.rearrange("p (a b c d) -> p a b c d", a=shape[0], b=shape[1], c=shape[2])
            return v

        qT = view(0, 8, S)
        kT = view(2048, 2, S)
        vv = view(2560, T, KVW)
        prob = [view(3072 + 2048 * u, 2, 4, 2 * P) for u in range(2)]
        pT = view(7168, 2, 2, 4, P)
        oT = view(9216, 8, S)
        aT = view(0, NFT, S)
        silu0 = view(5632, 2, S)
        poolT = view(0, KD, S)
        xg = view(0, KD, CAP)
        hid = view(768, FH)
        hidx = view(768 + FH, FH)
        hg = view(768 + 2 * FH, NI, P)
        hgx = view(768 + 3 * FH, NI, BASE)
        at = 768 + 3 * FH + NI * BASE
        sil = view(at, 2, FJ)
        silx = view(at + 2 * FJ, 2, FJ)
        y = view(at + 4 * FJ, 2, BANK)
        sc = view(at + 4 * FJ + 2 * BANK, 4, P)
        oddg = view(at + 4 * FJ + 3 * BANK, FJ)
        oddu = view(at + 5 * FJ + 3 * BANK, FJ)
        assert at + 6 * FJ + 3 * BANK <= 11264
        disp = sb("disp", [P, T, CAP])
        dispw = sb("dispw", [P, T, 2 * P])

        negm = sb("negm", [P, 2, 8])
        rsum = sb("rsum", [P, 2, 8])
        esink = sb("esink", [P, 2, 8])
        rden = sb("rden", [P, 2, 8])
        lg = sb("lg", [P, T, NE])
        top = sb("top", [P, T, 8])
        topi = sb("topi", [P, T, 8], U32)
        gate2 = sb("gate2", [P, T, 4])
        pick = sb("pick", [P, T, 2, NE])
        mask = sb("mask", [P, T, NE])
        comb = sb("comb", [P, T, NIT + 1])
        slot = sb("slot", [P, T, NIT + 1])
        cnt = sb("cnt", [P, NE])
        key = sb("key", [P, NE])
        ranked = sb("ranked", [P, NE])
        order = sb("order", [P, NE], U32)
        OVER, COL = NIT + 2, NIT + 3
        flagf = sb("flagf", [P, COL + NIT + 1])
        flags = sb("flags", [P, COL + NIT + 1], I32)

        x_in = [sem(f"x_in{t}") for t in range(T)]
        rows_in = sem("rows_in")
        bcast_in = sem("bcast_in")
        full = [sem(f"full{i}") for i in range(SLOTS)]
        pool_step = sem("pool_step")
        dve_step = sem("dve_step")
        act_step = sem("act_step")
        const_ready = sem("const_ready")
        band_counts = sem("band_counts")
        band_ready = sem("band_ready")
        ident_ready = sem("ident_ready")
        dist_ready = sem("dist_ready")
        zeros_ready = sem("zeros_ready")
        pw_scaled = sem("pw_scaled")
        egate_ready = sem("egate_ready")
        disp_part = sem("disp_part")
        gains_T = sem("gains_T")
        gains_ready = sem("gains_ready")
        std_ready = sem("std_ready")
        nrm_ready = sem("nrm_ready")
        x_ready = sem("x_ready")
        tr_done = sem("tr_done")
        hT_ready = sem("hT_ready")
        qkv_done = sem("qkv_done")
        q_ready = sem("q_ready")
        kv_ready = sem("kv_ready")
        s_done = sem("s_done")
        s_read = sem("s_read")
        negm_ready = sem("negm_ready")
        exp_done = sem("exp_done")
        prob_ready = sem("prob_ready")
        pt_done = sem("pt_done")
        pt_ready = sem("pt_ready")
        pv_done = sem("pv_done")
        o_ready = sem("o_ready")
        proj_done = sem("proj_done")
        gu_done = sem("gu_done")
        silu_ready = sem("silu_ready")
        a_ready = sem("a_ready")
        down0_done = sem("down0_done")
        pooled = sem("pooled")
        poolT_ready = sem("poolT_ready")
        mix_done = sem("mix_done")
        logits_done = sem("logits_done")
        mask_ready = sem("mask_ready")
        gap_ready = sem("gap_ready")
        rank_done = sem("rank_done")
        flags_ready = sem("flags_ready")
        disp_ready = sem("disp_ready")
        dispw_ready = sem("dispw_ready")
        gather_done = sem("gather_done")
        xg_ready = sem("xg_ready")
        gate_done = sem("gate_done")
        up_done = sem("up_done")
        gatex_done = sem("gatex_done")
        upx_done = sem("upx_done")
        oddg_ready = sem("oddg_ready")
        gatex_ready = sem("gatex_ready")
        oddu_ready = sem("oddu_ready")
        upx_ready = sem("upx_ready")
        sil_ready = sem("sil_ready")
        silx_ready = sem("silx_ready")
        hid_ready = sem("hid_ready")
        hidx_ready = sem("hidx_ready")
        htr_done = sem("htr_done")
        hxtr_done = sem("hxtr_done")
        hgA_ready = sem("hgA_ready")
        hgV_ready = sem("hgV_ready")
        hgxA_ready = sem("hgxA_ready")
        hgxV_ready = sem("hgxV_ready")
        down_done = sem("down_done")
        downx_done = sem("downx_done")
        y_ready = sem("y_ready")
        yx_ready = sem("yx_ready")
        ctr_done = sem("ctr_done")
        sc_ready = sem("sc_ready")
        scat_done = sem("scat_done")
        xadd_done = sem("xadd_done")
        out_ready = sem("out_ready")
        out_sent = sem("out_sent")
        rstd_ready = sem("rstd_ready")

        def out_rows(t):
            return hT[:, 4 * t:4 * t + 4, :].rearrange("p k s -> p (k s)")

        def cols(i, a, w):
            return ring[i][:, 0:a * w].rearrange("p (a w) -> p a w", a=a)

        wqkv = attn_w_qkv[0].rearrange("(k p) n -> p k n", p=P)
        wo = attn_w_o[0].rearrange("(m b i p) n -> m b p i n", m=2, b=2, i=4)
        wg0 = ffn_w_gate[0].rearrange("(k p) n -> p k n", p=P)
        wu0 = ffn_w_up[0].rearrange("(k p) n -> p k n", p=P)
        wd0 = ffn_w_down[0].rearrange("(k p) n -> p k n", p=P)
        pw = pool_w[0].rearrange("g (k p) n -> p (g k) n", p=P)
        stream = []
        for c in (2, 0, 1):
            stream.append([(cols(len(stream) % SLOTS, KD, BANK), wqkv[:, :, c * BANK:(c + 1) * BANK])])
        for m in range(2):
            dst = cols(len(stream) % SLOTS, 4, D)
            stream.append([(dst[64 * b:64 * b + 64], wo[m, b]) for b in range(2)])
        f = 0
        for n in FFN_TILES:
            for w in (wg0, wu0):
                stream.append([(cols(len(stream) % SLOTS, KD, n * P), w[:, :, f * P:(f + n) * P])])
            f += n
        f = 0
        for n in FFN_TILES:
            stream.append([(cols(len(stream) % SLOTS, n, D), wd0[:, f:f + n, :])])
            f += n
        stream.append([(cols(len(stream) % SLOTS, KD, 2 * P), pw)])
        assert len(stream) == C_MOE
        landed = [0] * SLOTS
        ready_at = []
        for n, parts in enumerate(stream):
            landed[n % SLOTS] += 16 * len(parts)
            ready_at.append((n % SLOTS, landed[n % SLOTS]))

        tiles = [sum(FFN_TILES[:j + 1]) for j in range(4)]
        read_by = [(qkv_done, 2), (qkv_done, 4), (qkv_done, 6), (proj_done, 1), (proj_done, 3)]
        read_by += [(gu_done, tiles[j]) for j in range(4) for _ in range(2)]
        read_by += [(down0_done, 1), (down0_done, 2), (down0_done, 3), (down0_done, 5), (mix_done, 2)]
        assert len(read_by) == C_MOE

        def moe_slot(c):
            return (C_MOE + c) % SLOTS

        def moe_full(it, c):
            return landed[moe_slot(c)] + 80 * it + (32, 64, 80)[c // SLOTS]

        block = ctx.enter_context(nc.Block())

        @block.sync
        def _(sp):
            xt = x[0].rearrange("(t p) d -> t p d", p=P)
            sp.dma_start(xres[:, 0, :], xt[0]).then_inc(x_in[0], 16)
            for i, g in enumerate((attn_norm, ffn_norm, pool_norm, moe_norm)):
                sp.dma_start(gain_rows[KD * i:KD * i + KD, :],
                             g[0].rearrange("(k p) -> k p", p=P)).then_inc(rows_in, 16)
            sp.dma_start(xres[:, 1, :], xt[1]).then_inc(x_in[1], 16)
            for n, parts in enumerate(stream):
                if n == 2:
                    for dst, src, w in ((sinks_b, attn_sinks[0:1, :], NH), (scale_b, pool_scale[0:1, :], D),
                                        (final_b, final_norm.rearrange("(a d) -> a d", a=1), D)):
                        sp.dma_start(dst[:, :], src.broadcast_to([P, w])).then_inc(bcast_in, 16)
                    sp.dma_start(router[:, :, :],
                                 moe_w_router[0].rearrange("(k p) e -> p k e", p=P)).then_inc(bcast_in, 16)
                if n >= SLOTS:
                    sp.wait_ge(*read_by[n - SLOTS])
                for dst, src in parts:
                    sp.dma_start(dst, src).then_inc(full[n % SLOTS], 16)

            def load_expert(it, e, first=False):
                for c in range(PER_IT):
                    if c >= SLOTS:
                        b = c - SLOTS
                        sp.wait_ge(up_done if b % 2 else gate_done, 4 * it + b // 2 + 1)
                        sp.wait_ge(upx_done if b % 2 else gatex_done, 4 * it + b // 2 + 1)
                    elif first:
                        sp.wait_ge(*read_by[C_MOE - SLOTS + c])
                    else:
                        sp.wait_ge(down_done, 4 * it + c - 3)
                        sp.wait_ge(downx_done, 4 * it + c - 3)
                    s = moe_slot(c)
                    if c < 8:
                        w = moe_w_up if c % 2 else moe_w_gate
                        w = w[0, bass.ds(e, 1)].rearrange("o (k p) (h j c) -> (o p) k h j c",
                                                          p=P, h=2, j=4)
                        dst = ring[s][:, :].rearrange("p (k h c) -> p k h c", k=KD, h=2)
                        for h in range(2):
                            sp.dma_start(dst[:, :, h, :], w[:, :, h, c // 2, :]).then_inc(full[s], 16)
                    else:
                        w = moe_w_down[0, bass.ds(e, 1)].rearrange("o (c i p) n -> (o p) c i n",
                                                                   p=P, i=ID)
                        sp.dma_start(cols(s, ID, D), w[:, c - 8]).then_inc(full[s], 16)

            load_expert(0, 0, first=True)
            sp.wait_ge(flags_ready, 1)
            with sp.Fori(1, NE, 1) as it:
                load_expert(it, sp.value_load(flags[0:1, bass.ds(it + COL, 1)], min_val=0, max_val=NE - 1))
            over = sp.value_load(flags[0:1, OVER:OVER + 1], min_val=0, max_val=1)
            with sp.If(over > 0):
                for r in range(1, ROUNDS):
                    with sp.Fori(0, NE, 1) as i:
                        load_expert(i + r * NE, sp.value_load(flags[0:1, bass.ds(i + COL, 1)],
                                                              min_val=0, max_val=NE - 1))
            with sp.Else():
                pass
            for t in range(T):
                sp.wait_ge(out_ready, 2 * t + 2)
                sp.dma_start(out[0].rearrange("(t p) d -> t p d", p=P)[t], out_rows(t)).then_inc(out_sent, 16)
            sp.wait_ge(out_sent, 16 * T)

        @block.gpsimd
        def _(pool):
            own = Steps(pool, pool_step)

            def select(t, pattern, base, mult, op, fill):
                own.link(nc.gpsimd.affine_select(out=t, in_=t, compare_op=op, fill=fill, base=base,
                                                 pattern=pattern, channel_multiplier=mult))

            own.step(nc.gpsimd.memset(eps_t[:, :], EPS))
            own.link(nc.gpsimd.memset(ident[:, :], 0.0))
            nc.gpsimd.affine_select(out=ident[:, :], in_=ident[:, :], compare_op=ALU.not_equal, fill=1.0,
                                    base=0, pattern=[[-1, P]], channel_multiplier=1).then_inc(ident_ready, 1)
            pool.wait_ge(ident_ready, 1)
            own.link(nc.gpsimd.iota(iota_i[:, :], pattern=[[-1, 2 * P]], base=P, channel_multiplier=1))
            own.link(nc.gpsimd.tensor_copy(dist[:, :], iota_i[:, :]))
            select(dist[:, :], [[-1, 2 * P]], P, 1, ALU.is_ge, FAR)
            select(dist[:, :], [[1, 2 * P]], -1, -1, ALU.is_ge, FAR)
            nc.gpsimd.memset(cnt[:, :], 0.0).then_inc(dist_ready, 1)
            own.step(nc.gpsimd.memset(ones[:, :], 1.0))
            own.link(nc.gpsimd.memset(upper[:, :], 1.0))
            select(upper[:, :], [[1, P]], 0, -1, ALU.is_gt, 0.0)
            own.link(nc.gpsimd.iota(iota_i[:, :], pattern=[[1, 2 * P]], base=0, channel_multiplier=0))
            own.link(nc.gpsimd.tensor_copy(iota_f[:, :], iota_i[:, :]))
            for b in (0, P + BASE):
                own.link(nc.gpsimd.tensor_copy(slot_id[:, b:b + BASE], iota_f[:, 0:BASE]))
            for b in range(BASE, P + BASE, EXT):
                own.link(nc.gpsimd.tensor_copy(slot_id[:, b:b + EXT], iota_f[:, BASE:CAP]))
            own.link(nc.gpsimd.memset(flagf[:, :], 0.0))
            nc.gpsimd.memset(flagf[:, COL + NIT:COL + NIT + 1], float(NIT)).then_inc(const_ready, 1)
            pool.wait_ge(band_counts, 1)
            for g, w in enumerate(WINDOWS):
                b0 = band[:, g, 0:S]
                b1 = band[:, g, S:S + P]
                for b, n in ((b0, S), (b1, P)):
                    select(b, [[1, n]], 0, -1, ALU.is_ge, 0.0)
                    select(b, [[-1, n]], w - 1, 1, ALU.is_ge, 0.0)
                    own.link(nc.gpsimd.tensor_tensor(b[:, 0:P], b[:, 0:P], ident[:, :], ALU.subtract))
            nc.gpsimd.memset(slot[:, :, NIT:NIT + 1], -1.0).then_inc(band_ready, 1)
            pool.wait_ge(x_ready, T)
            own.step(nc.gpsimd.memset(y[:, :, :], 0.0))
            own.step(nc.gpsimd.memset(comb[:, :, NIT:NIT + 1], 0.0))
            own.wait()
            nc.gpsimd.memset(sc[:, :, :], 0.0).then_inc(zeros_ready, 1)
            pool.wait_ge(zeros_ready, 1)
            for done, n in ((y_ready, 2), (yx_ready, 2), (sc_ready, 1), (ctr_done, 1), (xadd_done, 4)):
                pool.sem_inc(done, n)

        @block.scalar
        def _(act):
            own = Steps(act, act_step)
            def preload(func):
                own.wait()
                own.step(nc.scalar.activation(warm[:, :], eps_t[:, :], func))

            act.wait_ge(ident_ready, 1)
            own.step(nc.scalar.activation(warm[:, :], eps_t[:, :], ACT.Sqrt))

            def norm(q, t):
                if q == 0:
                    act.wait_ge(x_in[t], 16)
                else:
                    act.wait_ge(x_ready, T * (q - 1) + t + 1)
                own.link(nc.scalar.activation(nrm[:, t, :], xres[:, t, :], ACT.Square,
                                              accum_out=ssq[:, t:t + 1]))
                nc.scalar.activation(std[:, t:t + 1], ssq[:, t:t + 1], ACT.Sqrt, bias=eps_t[:, 0:1],
                                     scale=1.0 / D).then_inc(std_ready, 1)

            for t in range(T):
                norm(0, t)
            def queries(m):
                for i in (2 * m, 2 * m + 1):
                    act.wait_ge(qkv_done, i + 3)
                    nc.scalar.activation(qT[:, 2 * i:2 * i + 2, :],
                                         bank[4 + i][:, :].rearrange("p (a s) -> p a s", a=2),
                                         ACT.Copy, scale=HD ** -0.5).then_inc(q_ready, 1)

            queries(0)
            preload(ACT.Exp)

            def exps(u, n):
                act.wait_ge(negm_ready, u + 1)
                w0 = P if n == 0 else 0
                for h in range(8):
                    pr = prob[u % 2][:, h // 4, h % 4, w0:]
                    own.step(nc.scalar.activation(pr, pr, ACT.Exp, bias=negm[:, u % 2, h:h + 1],
                                                  accum_out=rsum[:, u % 2, h:h + 1]))
                nc.scalar.activation(esink[:, u % 2, :], esink[:, u % 2, :], ACT.Exp).then_inc(exp_done, 1)

            def keep_pT(u):
                if u >= 1:
                    act.wait_ge(pv_done, u)
                for bt, b, kt in batches_of(u):
                    act.wait_ge(pt_done, bt + 1)
                    nc.scalar.activation(pT[:, b, kt, :, :],
                                         bank[4 + bt % 2][:, :].rearrange("p (i q) -> p i q", i=4),
                                         ACT.Copy).then_inc(pt_ready, 1)

            def keep_o(u, m, n):
                act.wait_ge(pv_done, u + 1)
                nc.scalar.activation(oT[:, 4 * m:4 * m + 4, n * P:n * P + P],
                                     bank[6 + u % 2][:, :].rearrange("p (i q) -> p i q", i=4),
                                     ACT.Copy).then_inc(o_ready, 1)

            for u, (m, n) in enumerate(UNITS):
                if u % 2 == 0:
                    exps(u, UNITS[u][1])
                    exps(u + 1, UNITS[u + 1][1])
                keep_pT(u)
                if u == 0:
                    queries(1)
                keep_o(u, m, n)

            preload(ACT.Sqrt)
            for t in range(T):
                norm(1, t)
            preload(ACT.Silu)
            for u in range(NFT):
                act.wait_ge(gu_done, u + 1)
                if u >= 2:
                    act.wait_ge(a_ready, u - 1)
                nc.scalar.activation(silu0[:, u % 2, :], bank[u % 4][:, 0:S], ACT.Silu).then_inc(silu_ready, 1)
            preload(ACT.Sqrt)
            for q in (2, 3):
                for t in range(T):
                    norm(q, t)
            preload(ACT.Exp)
            act.wait_ge(gap_ready, 1)
            nc.scalar.activation(gate2[:, :, 1], gate2[:, :, 0], ACT.Exp).then_inc(egate_ready, 1)
            preload(ACT.Silu)
            act.wait_ge(flags_ready, 1)

            def expert(it):
                ext = act.value_load(flags[0:1, bass.ds(it + 1, 1)], min_val=0, max_val=1)
                for j in range(4):
                    act.wait_ge(gate_done, 4 * it + j + 1)
                    if j >= 2:
                        act.wait_ge(hid_ready, 4 * it + j - 1)
                    nc.scalar.activation(sil[:, j % 2, :], bank[2 * (j % 2)][:, 0:FJ],
                                         ACT.Silu).then_inc(sil_ready, 1)
                    with act.If(ext > 0):
                        act.wait_ge(gatex_done, 4 * it + j + 1)
                        if j >= 1:
                            act.wait_ge(silx_ready, 4 * it + j)
                        nc.scalar.activation(oddg[0:64, :], bank[4][64:128, 0:FJ],
                                             ACT.Copy).then_inc(oddg_ready, 1)
                        act.wait_ge(gatex_ready, 4 * it + j + 1)
                        if j >= 2:
                            act.wait_ge(hidx_ready, 4 * it + j - 1)
                        nc.scalar.activation(silx[0:64, j % 2, :], oddg[0:64, :],
                                             ACT.Silu).then_inc(silx_ready, 1)
                        act.wait_ge(upx_done, 4 * it + j + 1)
                        if j >= 1:
                            act.wait_ge(upx_ready, 4 * it + j)
                        nc.scalar.activation(oddu[0:64, :], bank[5][64:128, 0:FJ],
                                             ACT.Copy).then_inc(oddu_ready, 1)
                    with act.Else():
                        act.sem_inc(oddg_ready, 1)
                        act.sem_inc(silx_ready, 1)
                        act.sem_inc(oddu_ready, 1)
                for b in (0, 2):
                    act.wait_ge(htr_done, 4 * it + b + 1)
                    i, n = 4 * b, min(4, NI - 4 * b)
                    nc.scalar.activation(hg[:, i:i + n, :],
                                         bank[HTR_BANK[b]][:, 0:n * P].rearrange("p (i s) -> p i s", i=n),
                                         ACT.Copy).then_inc(hgA_ready, 1)
                with act.If(ext > 0):
                    act.wait_ge(hxtr_done, 2 * it + 1)
                    nc.scalar.activation(hgx[:, 0:7, :],
                                         bank[6][:, 0:7 * 64].rearrange("p (i s) -> p i s", i=7),
                                         ACT.Copy).then_inc(hgxA_ready, 1)
                with act.Else():
                    act.sem_inc(hgxA_ready, 1)
                act.wait_ge(ctr_done, it + 2)
                nc.scalar.activation(sc[:, :, :], bank[4][:, :].rearrange("p (a q) -> p a q", a=4),
                                     ACT.Copy).then_inc(sc_ready, 1)
                act.wait_ge(down_done, 4 * it + 4)
                nc.scalar.activation(y[0:64, 0, :], bank[2][0:64, :], ACT.Copy).then_inc(y_ready, 1)

            with act.Fori(0, NE, 1) as it:
                expert(it)
            over = act.value_load(flags[0:1, OVER:OVER + 1], min_val=0, max_val=1)
            with act.If(over > 0):
                with act.Fori(NE, NIT, 1) as it:
                    expert(it)
            with act.Else():
                pass
            preload(ACT.Sqrt)
            for t in range(T):
                norm(4, t)
                act.wait_ge(rstd_ready, t + 1)
                nc.scalar.activation(out_rows(t)[:, BANK:D], out_rows(t)[:, BANK:D], ACT.Copy,
                                     scale=rstd[:, t:t + 1]).then_inc(out_ready, 1)

        @block.vector
        def _(dve):
            own = Steps(dve, dve_step)

            def norm(q, t):
                dve.wait_ge(std_ready, T * q + t + 1)
                own.link(nc.vector.reciprocal(rstd[:, t:t + 1], std[:, t:t + 1]))
                nc.vector.tensor_scalar(nrm[:, t, :], xres[:, t, :], rstd[:, t:t + 1], None,
                                        ALU.mult).then_inc(nrm_ready, 1)

            def gained(dst, src, gi, n):
                g = gains[:, gi:gi + n].rearrange("p (k o) -> p k o", o=1)
                return nc.vector.tensor_tensor(dst, src, g.broadcast_to([P, n, dst.shape[2]]), ALU.mult)

            def keep_hT(t, gi, banks, first):
                for kh in range(2):
                    n = 2 * t + kh
                    dve.wait_ge(tr_done, first + n + 1)
                    gained(hT[:, 4 * kh:4 * kh + 4, t * P:t * P + P],
                           bank[banks + n][:, :].rearrange("p (k s) -> p k s", k=4),
                           gi + 4 * kh, 4).then_inc(hT_ready, 1)

            def add_x(t, banks, wait, value):
                dve.wait_ge(wait, value)
                for h in range(2):
                    xs = xres[:, t, h * BANK:h * BANK + BANK]
                    ins = nc.vector.tensor_tensor(xs, bank[banks + 2 * t + h][:, :], xs, ALU.add)
                    if h == 0:
                        own.step(ins)
                    else:
                        own.wait()
                        ins.then_inc(x_ready, 1)

            norm(0, 0)
            norm(0, 1)
            dve.wait_ge(gains_T, 1)
            nc.vector.tensor_copy(gains[:, :], bank[7][:, 0:4 * KD]).then_inc(gains_ready, 1)
            dve.wait_ge(gains_ready, 1)
            for t in range(T):
                keep_hT(t, 0, 0, 0)
            dve.wait_ge(qkv_done, 1)
            nc.vector.tensor_copy(kT[:, :, :], bank[0][:, :].rearrange("p (m s) -> p m s", m=2)).then_inc(kv_ready, 1)
            dve.wait_ge(qkv_done, 2)
            nc.vector.tensor_copy(vv[:, :, :], bank[1][:, :].rearrange("p (t c) -> p t c", t=2)).then_inc(kv_ready, 1)
            dve.wait_ge(bcast_in, 64)
            dve.wait_ge(const_ready, 1)
            for g, w in enumerate(WINDOWS):
                own.step(nc.vector.tensor_scalar(band[:, g, 0:S], iota_f[:, :], 1.0, float(w),
                                                 ALU.add, ALU.min))
                own.step(nc.vector.memset(band[:, g, S:S + P], 1.0 / w))
            own.wait()
            nc.vector.reciprocal(band[:, :, 0:S], band[:, :, 0:S]).then_inc(band_counts, 1)
            dve.wait_ge(dist_ready, 1)

            def scores(u, m, n):
                w0 = P if n == 0 else 0
                pr = prob[u % 2]
                dve.wait_ge(s_done, u + 1)
                if u >= 2:
                    dve.wait_ge(pt_done, batches_of(u - 2)[-1][0] + 1)
                for h in range(8):
                    slope = 2.0 ** (-8.0 * (8 * m + h + 1) / NH)
                    ins = nc.vector.scalar_tensor_tensor(
                        out=pr[:, h // 4, h % 4, w0:], in0=dist[:, w0:], scalar=-slope,
                        in1=bank[h // 2][:, (h % 2) * 2 * P + w0:(h % 2 + 1) * 2 * P],
                        op0=ALU.mult, op1=ALU.add)
                    if h < 7:
                        own.step(ins)
                    else:
                        ins.then_inc(s_read, 1)
                own.wait()
                dve.wait_ge(s_read, u + 1)
                nm, es, sk = negm[:, u % 2, :], esink[:, u % 2, :], sinks_b[:, 8 * m:8 * m + 8]
                own.link(nc.vector.reduce_max(nm, pr[:, :, :, w0:].rearrange("p b i k -> p (b i) k"), axis=AX_X))
                own.link(nc.vector.tensor_tensor(nm, nm, sk, ALU.max))
                own.link(nc.vector.tensor_scalar(nm, nm, -1.0, None, ALU.mult))
                nc.vector.tensor_tensor(es, sk, nm, ALU.add).then_inc(negm_ready, 1)

            def normalise(u, n):
                w0 = P if n == 0 else 0
                dve.wait_ge(exp_done, u + 1)
                rd = rden[:, u % 2, :]
                own.link(nc.vector.tensor_tensor(rd, rsum[:, u % 2, :], esink[:, u % 2, :], ALU.add))
                own.link(nc.vector.reciprocal(rd, rd))
                pr = prob[u % 2][:, :, :, w0:].rearrange("p b i k -> p (b i) k")
                r = rd.rearrange("p (h o) -> p h o", o=1).broadcast_to([P, 8, 2 * P - w0])
                nc.vector.tensor_tensor(pr, pr, r, ALU.mult).then_inc(prob_ready, 1)

            for u in (0, 2):
                scores(u, *UNITS[u])
                scores(u + 1, *UNITS[u + 1])
                normalise(u, UNITS[u][1])
                normalise(u + 1, UNITS[u + 1][1])
            for t in range(T):
                add_x(t, 0, proj_done, t + 2)
                norm(1, t)
                keep_hT(t, KD, 4, 2 * T)
            for u in range(NFT):
                dve.wait_ge(silu_ready, u + 1)
                nc.vector.tensor_tensor(aT[:, u, :], bank[u % 4][:, S:2 * S], silu0[:, u % 2, :],
                                        ALU.mult).then_inc(a_ready, 1)
            dve.wait_ge(full[ready_at[C_POOL][0]], ready_at[C_POOL][1])
            maps = stream[C_POOL][0][0].rearrange("p (g k) c -> p g k c", k=2)
            for k in range(2):
                own.step(nc.vector.tensor_tensor(maps[:, :, k, :], maps[:, :, k, :],
                                                 scale_b[:, :].rearrange("p (g c) -> p g c", g=4), ALU.mult))
            own.wait()
            dve.sem_inc(pw_scaled, 1)
            def keep_poolT(t):
                for kh in range(2):
                    dve.wait_ge(pooled, 2 * t + kh + 1)
                    gained(poolT[:, 4 * kh:4 * kh + 4, t * P:t * P + P],
                           bank[2 * t + kh][:, :].rearrange("p (k s) -> p k s", k=4),
                           2 * KD + 4 * kh, 4).then_inc(poolT_ready, 1)

            add_x(0, 4, down0_done, 4)
            norm(2, 0)
            add_x(1, 4, down0_done, 5)
            keep_poolT(0)
            norm(2, 1)
            keep_poolT(1)
            add_x(0, 4, mix_done, 1)
            norm(3, 0)
            add_x(1, 4, mix_done, 2)
            keep_hT(0, 3 * KD, 0, 4 * T)
            norm(3, 1)
            keep_hT(1, 3 * KD, 0, 4 * T)

            dve.wait_ge(band_ready, 1)
            cols8 = iota_f[:, 0:NE].rearrange("p (t e) -> p t e", t=1).broadcast_to([P, T, NE])
            for t in range(T):
                dve.wait_ge(logits_done, t + 1)
                own.link(nc.vector.tensor_copy(lg[:, t, :], bank[4 + t][:, 0:NE]))
                own.link(nc.vector.max(top[:, t, :], lg[:, t, :]))
                own.link(nc.vector.max_index(topi[:, t, :], top[:, t, :], lg[:, t, :]))
                own.link(nc.vector.tensor_tensor(
                    pick[:, t, :, :], cols8,
                    topi[:, t, 0:2].rearrange("p (j o) -> p j o", o=1).broadcast_to([P, T, NE]), ALU.is_equal))
                nc.vector.tensor_tensor(mask[:, t, :], pick[:, t, 0, :], pick[:, t, 1, :],
                                        ALU.add).then_inc(mask_ready, 1)
            nc.vector.tensor_tensor(gate2[:, :, 0], top[:, :, 1], top[:, :, 0],
                                    ALU.subtract).then_inc(gap_ready, 1)
            dve.wait_ge(mask_ready, 2)
            dve.wait_ge(rank_done, 1)
            own.link(nc.vector.scalar_tensor_tensor(
                out=slot[:, :, 0:NE], in0=bank[0][:, 0:T * NE].rearrange("p (t e) -> p t e", t=T),
                scalar=1000.0, in1=mask[:, :, :], op0=ALU.add, op1=ALU.mult))
            own.link(nc.vector.tensor_scalar(slot[:, :, 0:NE], slot[:, :, 0:NE], -1000.0, None, ALU.add))
            def column(it):
                return dve.value_load(flags[0:1, bass.ds(it + COL, 1)], min_val=0, max_val=NIT)

            def dispatch(col):
                for t in range(T):
                    nc.vector.tensor_scalar(disp[:, t, :], iota_f[:, 0:CAP], slot[:, t, bass.ds(col, 1)],
                                            None, ALU.is_equal).then_inc((disp_part, disp_ready)[t], 1)

            def keep_xg(n):
                for h in range(2):
                    dve.wait_ge(gather_done, 2 * n + h - 1)
                    ins = gained(xg[:, 4 * h:4 * h + 4, :],
                                 bank[6 + h][:, 0:4 * CAP].rearrange("p (k s) -> p k s", k=4),
                                 3 * KD + 4 * h, 4)
                    ins.then_inc(xg_ready, 1)

            def scattered(n, t, banks=6):
                for h in range(2):
                    dve.wait_ge(scat_done, 2 * (n * T + t) + h + 1)
                    hs = slice(h * BANK, h * BANK + BANK)
                    nc.vector.tensor_tensor(xres[:, t, hs], bank[banks + h][:, :], xres[:, t, hs],
                                            ALU.add).then_inc(xadd_done, 1)

            dispatch(0)
            dve.wait_ge(egate_ready, 1)
            own.link(nc.vector.tensor_scalar(gate2[:, :, 2], gate2[:, :, 1], 1.0, None, ALU.add))
            own.link(nc.vector.reciprocal(gate2[:, :, 2], gate2[:, :, 2]))
            own.link(nc.vector.tensor_tensor(gate2[:, :, 3], gate2[:, :, 1], gate2[:, :, 2], ALU.mult))
            for t in range(T):
                own.link(nc.vector.tensor_scalar(comb[:, t, 0:NE], pick[:, t, 0, :], gate2[:, t, 2:3],
                                                 None, ALU.mult))
                own.link(nc.vector.scalar_tensor_tensor(
                    out=comb[:, t, 0:NE], in0=pick[:, t, 1, :], scalar=gate2[:, t, 3:4],
                    in1=comb[:, t, 0:NE], op0=ALU.mult, op1=ALU.add))
            for r in range(1, ROUNDS):
                own.step(nc.vector.tensor_copy(comb[:, :, r * NE:r * NE + NE], comb[:, :, 0:NE]))
                own.step(nc.vector.tensor_scalar(slot[:, :, r * NE:r * NE + NE], slot[:, :, 0:NE],
                                                 float(CAP * r), None, ALU.subtract))
            dve.wait_ge(rank_done, 2)
            own.link(nc.vector.tensor_copy(cnt[:, :], bank[1][:, 0:NE]))
            own.link(nc.vector.scalar_tensor_tensor(out=key[:, :], in0=iota_f[:, 0:NE], scalar=-1.0 / 16,
                                                    in1=cnt[:, :], op0=ALU.mult, op1=ALU.add))
            own.link(nc.vector.tensor_scalar(key[:, 0:1], key[:, 0:1], 1000.0, None, ALU.add))
            own.link(nc.vector.max(ranked[:, :], key[:, :]))
            own.link(nc.vector.max_index(order[:, :], ranked[:, :], key[:, :]))
            own.link(nc.vector.tensor_scalar(ranked[:, 0:1], ranked[:, 0:1], -1000.0, None, ALU.add))
            for r in range(ROUNDS):
                own.step(nc.vector.tensor_scalar(flagf[:, COL + r * NE:COL + r * NE + NE], order[:, :],
                                                 float(r * NE), None, ALU.add))
                own.step(nc.vector.tensor_scalar(flagf[:, 1 + r * NE:1 + r * NE + NE], ranked[:, :],
                                                 CAP * r + BASE + 0.5, None, ALU.is_gt))
            own.link(nc.vector.reduce_max(flagf[:, OVER:OVER + 1], cnt[:, :], axis=AX_X))
            own.link(nc.vector.tensor_scalar(flagf[:, OVER:OVER + 1], flagf[:, OVER:OVER + 1],
                                             float(CAP), None, ALU.is_gt))
            nc.vector.tensor_copy(flags[:, :], flagf[:, :]).then_inc(flags_ready, 1)
            keep_xg(1)
            dve.wait_ge(flags_ready, 1)
            dve.wait_ge(zeros_ready, 1)

            def expert(it):
                ext = dve.value_load(flags[0:1, bass.ds(it + 1, 1)], min_val=0, max_val=1)
                dve.wait_ge(ctr_done, it + 1)
                col = column(it)
                dve.wait_ge(xadd_done, 4 * it + 4)
                for t in range(T):
                    nc.vector.tensor_scalar(dispw[:, t, :], slot_id[:, :], slot[:, t, bass.ds(col, 1)],
                                            comb[:, t, bass.ds(col, 1)], ALU.is_equal,
                                            ALU.mult).then_inc(dispw_ready, 1)
                for j in range(4):
                    js = slice(j * FJ, j * FJ + FJ)
                    with dve.If(ext > 0):
                        dve.wait_ge(oddg_ready, 4 * it + j + 1)
                        nc.vector.tensor_tensor(oddg[0:64, :], bank[4][0:64, 0:FJ], oddg[0:64, :],
                                                ALU.add).then_inc(gatex_ready, 1)
                    with dve.Else():
                        dve.sem_inc(gatex_ready, 1)
                    dve.wait_ge(up_done, 4 * it + j + 1)
                    dve.wait_ge(sil_ready, 4 * it + j + 1)
                    nc.vector.tensor_tensor(hid[:, js], bank[2 * (j % 2) + 1][:, 0:FJ], sil[:, j % 2, :],
                                            ALU.mult).then_inc(hid_ready, 1)
                    with dve.If(ext > 0):
                        dve.wait_ge(oddu_ready, 4 * it + j + 1)
                        nc.vector.tensor_tensor(hidx[0:64, js], bank[5][0:64, 0:FJ], oddu[0:64, :],
                                                ALU.add).then_inc(upx_ready, 1)
                        dve.wait_ge(silx_ready, 4 * it + j + 1)
                        dve.wait_ge(upx_ready, 4 * it + j + 1)
                        nc.vector.tensor_tensor(hidx[0:64, js], hidx[0:64, js], silx[0:64, j % 2, :],
                                                ALU.mult).then_inc(hidx_ready, 1)
                    with dve.Else():
                        dve.sem_inc(upx_ready, 1)
                        dve.sem_inc(hidx_ready, 1)
                    if j < 2:
                        scattered(it, j)
                    if j == 1:
                        dve.wait_ge(gather_done, 2 * it + 2)
                        dispatch(column(it + 1))
                keep_xg(it + 2)
                for b in (1, 3):
                    i, n = 4 * b, min(4, NI - 4 * b)
                    dve.wait_ge(htr_done, 4 * it + b + 1)
                    nc.vector.tensor_copy(hg[:, i:i + n, :],
                                          bank[HTR_BANK[b]][:, 0:n * P].rearrange("p (i s) -> p i s", i=n)
                                          ).then_inc(hgV_ready, 1)
                with dve.If(ext > 0):
                    dve.wait_ge(hxtr_done, 2 * it + 2)
                    nc.vector.tensor_copy(hgx[:, 7:14, :],
                                          bank[7][:, 0:7 * 64].rearrange("p (i s) -> p i s", i=7)
                                          ).then_inc(hgxV_ready, 1)
                with dve.Else():
                    dve.sem_inc(hgxV_ready, 1)
                dve.wait_ge(down_done, 4 * it + 4)
                nc.vector.tensor_copy(y[64:128, 1, :], bank[2][64:128, :]).then_inc(y_ready, 1)
                with dve.If(ext > 0):
                    dve.wait_ge(downx_done, 4 * it + 4)
                    for h in range(2):
                        hp = slice(64 - 64 * h, 128 - 64 * h)
                        nc.vector.tensor_copy(y[hp, h, :], bank[3][hp, :]).then_inc(yx_ready, 1)
                with dve.Else():
                    dve.sem_inc(yx_ready, 2)

            def final(n, t):
                if t == 0:
                    dve.wait_ge(xadd_done, 4 * n + 4)
                scattered(n, t, (6, 0)[t])
                dve.wait_ge(xadd_done, 4 * n + 2 * t + 6)
                dve.sem_inc(x_ready, 1)

            with dve.Fori(0, NE, 1) as it:
                expert(it)
            over = dve.value_load(flags[0:1, OVER:OVER + 1], min_val=0, max_val=1)
            with dve.If(over > 0):
                with dve.Fori(NE, NIT, 1) as it:
                    expert(it)
                final(NIT, 0)
            with dve.Else():
                final(NE, 0)
            dve.wait_ge(x_ready, 3 * T + 1)
            own.step(nc.vector.tensor_tensor(out_rows(0), xres[:, 0, :], final_b[:, :], ALU.mult))
            with dve.If(over > 0):
                final(NIT, 1)
            with dve.Else():
                final(NE, 1)
            dve.wait_ge(x_ready, 3 * T + 2)
            for t in range(T):
                if t == 1:
                    own.step(nc.vector.tensor_tensor(out_rows(1), xres[:, 1, :], final_b[:, :], ALU.mult))
                dve.wait_ge(std_ready, 4 * T + t + 1)
                own.wait()
                nc.vector.reciprocal(rstd[:, t:t + 1], std[:, t:t + 1]).then_inc(rstd_ready, 1)
                dve.wait_ge(rstd_ready, t + 1)
                nc.vector.tensor_scalar(out_rows(t)[:, 0:BANK], out_rows(t)[:, 0:BANK], rstd[:, t:t + 1],
                                        None, ALU.mult).then_inc(out_ready, 1)

        @block.tensor
        def _(pe):
            mm = nc.tensor.matmul

            def chunk_landed(n):
                pe.wait_ge(full[ready_at[n][0]], ready_at[n][1])

            def transposes(q, banks, ts=range(T)):
                for t in ts:
                    pe.wait_ge(nrm_ready, T * q + t + 1)
                    for kh in range(2):
                        for k in range(4):
                            c = (4 * kh + k) * P
                            last = nc.tensor.transpose(bank[banks + 2 * t + kh][:, k * P:k * P + P],
                                                       nrm[:, t, c:c + P], ident[:, :])
                        last.then_inc(tr_done, 1)

            pe.wait_ge(ident_ready, 1)
            pe.wait_ge(rows_in, 64)
            nc.tensor.transpose(bank[7][:, 0:4 * KD], gain_rows[:, :],
                                ident[0:4 * KD, 0:4 * KD]).then_inc(gains_T, 1)
            transposes(0, 0)
            pe.wait_ge(hT_ready, 2 * T)
            pe.wait_ge(gains_ready, 1)
            chunk_landed(C_QKV)
            w = stream[C_QKV][0][0]
            for m in range(2):
                for k in range(KD):
                    last = mm(bank[0][:, m * S:m * S + S], w[:, k, m * P:m * P + P], hT[:, k, :],
                              start=k == 0, stop=k == KD - 1)
            last.then_inc(qkv_done, 1)
            for t in range(T):
                for k in range(KD):
                    last = mm(bank[1][:, t * KVW:t * KVW + KVW], hT[:, k, t * P:t * P + P],
                              w[:, k, KVW:2 * KVW], start=k == 0, stop=k == KD - 1)
            last.then_inc(qkv_done, 1)

            def queries(m, pairs=range(4)):
                chunk_landed(C_QKV + 1 + m)
                w = stream[C_QKV + 1 + m][0][0]
                for i in pairs:
                    for k in range(KD):
                        for b in range(2):
                            c = (4 * b + i) * HD
                            last = mm(bank[4 + 2 * m + i // 2][64 * b:64 * b + 64, (i % 2) * S:(i % 2) * S + S],
                                      w[:, k, c:c + HD], hT[:, k, :], start=k == 0, stop=k == KD - 1)
                    if i % 2:
                        last.then_inc(qkv_done, 1)

            def scores(u, m, n):
                pe.wait_ge(q_ready, 2 * m + 2)
                if u == 0:
                    pe.wait_ge(kv_ready, 2)
                else:
                    pe.wait_ge(s_read, u)
                w0 = P if n == 0 else 0
                for i in range(4):
                    for b in range(2):
                        last = mm(bank[2 * b + i // 2][:, (i % 2) * 2 * P + w0:(i % 2 + 1) * 2 * P],
                                  qT[64 * b:64 * b + 64, 4 * m + i, n * P:n * P + P],
                                  kT[64 * b:64 * b + 64, m, 0:2 * P - w0], start=True, stop=True)
                last.then_inc(s_done, 1)

            def keys_down(u):
                pe.wait_ge(prob_ready, u + 1)
                for bt, b, kt in batches_of(u):
                    if bt >= 2:
                        pe.wait_ge(pt_ready, bt - 1)
                    else:
                        pe.wait_ge(q_ready, 2)
                    for i in range(4):
                        last = nc.tensor.transpose(bank[4 + bt % 2][:, i * P:i * P + P],
                                                   prob[u % 2][:, b, i, kt * P:kt * P + P], ident[:, :])
                    last.then_inc(pt_done, 1)

            def values(u, m, n):
                if u < 2:
                    pe.wait_ge(q_ready, 4)
                else:
                    pe.wait_ge(o_ready, u - 1)
                pe.wait_ge(pt_ready, batches_of(u)[-1][0] + 1)
                kts = (1,) if n == 0 else (0, 1)
                for kt in kts:
                    for b in range(2):
                        g = 2 * m + b
                        last = mm(bank[6 + u % 2][64 * b:64 * b + 64, :],
                                  vv[:, n - 1 + kt, g * HD:g * HD + HD],
                                  pT[:, b, kt, :, :].rearrange("p i q -> p (i q)"),
                                  start=kt == kts[0], stop=kt == 1)
                last.then_inc(pv_done, 1)

            def project(m, t, tiles_of_block=range(4)):
                pe.wait_ge(o_ready, 2 * m + 2)
                chunk_landed(C_WO + m)
                w = cols((C_WO + m) % SLOTS, 4, D)
                for i in tiles_of_block:
                    for h in range(2):
                        last = mm(bank[2 * t + h][:, :], oT[:, 4 * m + i, t * P:t * P + P],
                                  w[:, i, h * BANK:h * BANK + BANK], start=m == 0 and i == 0,
                                  stop=m == 1 and i == 3)
                if i == 3 and (m == 1 or t == 1):
                    last.then_inc(proj_done, 1)

            queries(0)
            scores(0, *UNITS[0])
            scores(1, *UNITS[1])
            queries(1, (0, 1))
            keys_down(0)
            queries(1, (2, 3))
            values(0, *UNITS[0])
            scores(2, *UNITS[2])
            keys_down(1)
            scores(3, *UNITS[3])
            values(1, *UNITS[1])
            pe.wait_ge(s_read, 4)
            project(0, 0)
            keys_down(2)
            project(0, 1, (0, 1))
            values(2, *UNITS[2])
            keys_down(3)
            project(0, 1, (2, 3))
            values(3, *UNITS[3])
            project(1, 0)
            project(1, 1, (0, 1))
            transposes(1, 4, (0,))
            project(1, 1, (2, 3))

            def unit(u, ts):
                j = next(i for i in range(4) if u < tiles[i])
                f = (u - tiles[j] + FFN_TILES[j]) * P
                for half in range(2):
                    w = stream[C_FFN + 2 * j + half][0][0]
                    for k in range(KD):
                        last = mm(bank[u % 4][:, half * S + ts.start:half * S + ts.stop], w[:, k, f:f + P],
                                  hT[:, k, ts], start=k == 0, stop=k == KD - 1)
                return last

            chunk_landed(C_FFN)
            chunk_landed(C_FFN + 1)
            pe.wait_ge(x_ready, 1)
            pe.wait_ge(hT_ready, 2 * T + 2)
            for u in range(2):
                if u == 1:
                    transposes(1, 4, (1,))
                unit(u, slice(0, P))
            pe.wait_ge(hT_ready, 4 * T)
            for u in range(2):
                unit(u, slice(P, S)).then_inc(gu_done, 1)
            for u in range(2, NFT):
                if u in tiles:
                    c = C_FFN + 2 * tiles.index(u) + 2
                    chunk_landed(c)
                    chunk_landed(c + 1)
                if u >= 4:
                    pe.wait_ge(a_ready, u - 3)
                unit(u, slice(0, S)).then_inc(gu_done, 1)
            u = 0
            for j, n in enumerate(FFN_TILES):
                pe.wait_ge(a_ready, tiles[j])
                c = C_FFN + 8 + j
                chunk_landed(c)
                w = stream[c][0][0]
                order = [(t, f) for f in range(n) for t in range(T)]
                if j == 3:
                    order.sort()
                for t, f in order:
                    for h in range(2):
                        last = mm(bank[4 + 2 * t + h][:, :], aT[:, u + f, t * P:t * P + P],
                                  w[:, f, h * BANK:h * BANK + BANK], start=u + f == 0, stop=u + f == NFT - 1)
                    if j == 3 and f == n - 1 and t == 0:
                        last.then_inc(down0_done, 1)
                last.then_inc(down0_done, 1)
                u += n

            def pool_mix(t, src):
                for kh in range(2):
                    for k in range(4):
                        c = 4 * kh + k
                        b0 = S if src == 1 else t * P
                        last = mm(bank[2 * t + kh][:, k * P:k * P + P], nrm[:, src, c * P:c * P + P],
                                  band[:, c // 2, b0:b0 + P], start=src == 0 and k == 0,
                                  stop=src == t and k == 3)
                    if src == t:
                        last.then_inc(pooled, 1)

            pe.wait_ge(nrm_ready, 2 * T + 1)
            pe.wait_ge(band_ready, 1)
            pool_mix(0, 0)
            pool_mix(1, 0)
            pe.wait_ge(pw_scaled, 1)
            w = stream[C_POOL][0][0]

            def map_groups(t, groups):
                for g in groups:
                    for k in range(2):
                        last = mm(bank[4 + 2 * t + g // 2][:, (g % 2) * 2 * P:(g % 2 + 1) * 2 * P],
                                  poolT[:, 2 * g + k, t * P:t * P + P], w[:, 2 * g + k, :],
                                  start=k == 0, stop=k == 1)
                if groups[-1] == 3:
                    last.then_inc(mix_done, 1)

            pe.wait_ge(poolT_ready, 1)
            map_groups(0, (0, 1))
            pe.wait_ge(nrm_ready, 2 * T + 2)
            pool_mix(1, 1)
            pe.wait_ge(poolT_ready, 2)
            map_groups(0, (2, 3))
            pe.wait_ge(poolT_ready, 4)
            map_groups(1, (0, 1, 2, 3))

            pe.wait_ge(bcast_in, 64)
            pe.wait_ge(const_ready, 1)
            for t in range(T):
                transposes(3, 0, (t,))
                pe.wait_ge(hT_ready, 4 * T + 2 * t + 2)
                for k in range(KD):
                    last = mm(bank[4 + t][:, 0:NE], hT[:, k, t * P:t * P + P], router[:, k, :],
                              start=k == 0, stop=k == KD - 1)
                last.then_inc(logits_done, 1)
            pe.wait_ge(mask_ready, 1)
            mm(bank[0][:, 0:NE], upper[:, :], mask[:, 0, :], start=True, stop=True)
            mm(bank[0][:, NE:2 * NE], ones[:, :], mask[:, 0, :], start=True, stop=False)
            pe.wait_ge(mask_ready, 2)
            mm(bank[0][:, NE:2 * NE], upper[:, :], mask[:, 1, :], start=False, stop=True).then_inc(rank_done, 1)
            mm(bank[1][:, 0:NE], ones[:, :], mask[:, 0, :], start=True, stop=False)
            mm(bank[1][:, 0:NE], ones[:, :], mask[:, 1, :], start=False, stop=True).then_inc(rank_done, 1)

            def gather(n):
                pe.wait_ge(disp_ready, n)
                pe.wait_ge(disp_part, n)
                for k in range(KD):
                    for t in range(T):
                        last = mm(bank[6 + k // 4][:, (k % 4) * CAP:(k % 4) * CAP + CAP],
                                  nrm[:, t, k * P:k * P + P], disp[:, t, :], start=t == 0, stop=t == 1)
                    if k % 4 == 3:
                        last.then_inc(gather_done, 1)

            def scatter(ext, n, t, banks):
                with pe.If(ext > 0):
                    for h in range(2):
                        mm(bank[banks + h][:, :], sc[:, T * h + t, :], y[:, h, :],
                           start=True, stop=True).then_inc(scat_done, 1)
                with pe.Else():
                    for h in range(2):
                        hp = slice(64 * h, 64 * h + 64)
                        mm(bank[banks + h][:, :], sc[hp, T * h + t, :], y[hp, h, :],
                           start=True, stop=True).then_inc(scat_done, 1)

            def gate_up(it, j, ext):
                for up in range(2):
                    c = 2 * j + up
                    pe.wait_ge(full[moe_slot(c)], moe_full(it, c))
                    if j >= 2:
                        pe.wait_ge(hid_ready if up else sil_ready, 4 * it + j - 1)
                    elif j == 1:
                        pe.wait_ge(yx_ready if up else y_ready, 2 * it + 2)
                    w = ring[moe_slot(c)][:, :].rearrange("p (k h c) -> p k h c", k=KD, h=2)
                    for k in range(KD):
                        if j == 0 and up == 0 and k % 4 == 0:
                            pe.wait_ge(xg_ready, 2 * it + k // 4 + 1)
                        for h in range(2):
                            last = mm(bank[2 * (j % 2) + up][64 * h:64 * h + 64, 0:FJ], xg[:, k, 0:BASE],
                                      w[:, k, h, :], start=k == 0, stop=k == KD - 1)
                    last.then_inc(up_done if up else gate_done, 1)
                    with pe.If(ext > 0):
                        if j >= 1:
                            pe.wait_ge(upx_ready if up else gatex_ready, 4 * it + j)
                        elif not up:
                            pe.wait_ge(sc_ready, it + 1)
                        for k in range(KD):
                            for h in range(2):
                                q = 64 * (k % 2) + 32 * h
                                last = mm(bank[4 + up][q:q + 32, 0:FJ], xg[:, k, BASE:CAP], w[:, k, h, :],
                                          start=k < 2, stop=k >= KD - 2)
                        last.then_inc(upx_done if up else gatex_done, 1)
                    with pe.Else():
                        pe.sem_inc(upx_done if up else gatex_done, 1)

            def expert(it):
                extp = pe.value_load(flags[0:1, bass.ds(it, 1)], min_val=0, max_val=1)
                ext = pe.value_load(flags[0:1, bass.ds(it + 1, 1)], min_val=0, max_val=1)
                gate_up(it, 0, ext)
                pe.wait_ge(y_ready, 2 * it + 2)
                pe.wait_ge(yx_ready, 2 * it + 2)
                pe.wait_ge(sc_ready, it + 1)
                scatter(extp, it, 0, 6)
                gate_up(it, 1, ext)
                pe.wait_ge(xadd_done, 4 * it + 6)
                scatter(extp, it, 1, 6)
                gate_up(it, 2, ext)
                gate_up(it, 3, ext)
                pe.wait_ge(xadd_done, 4 * it + 8)
                gather(it + 2)
                for b in range(4):
                    pe.wait_ge(hid_ready, 4 * it + min(b + 3, 4) if b < 2 else 4 * it + 4)
                    if b >= 2:
                        pe.wait_ge(hidx_ready, 4 * it + 4)
                    for i in range(4 * b, min(4 * b + 4, NI)):
                        last = nc.tensor.transpose(bank[HTR_BANK[b]][:, (i % 4) * P:(i % 4) * P + P],
                                                   hid[:, i * P:i * P + P], ident[:, :])
                    last.then_inc(htr_done, 1)
                pe.wait_ge(xg_ready, 2 * it + 4)
                with pe.If(ext > 0):
                    for b in range(2):
                        for i in range(7):
                            c = (7 * b + i) * P
                            last = nc.tensor.transpose(bank[6 + b][:, i * 64:i * 64 + 64],
                                                       hidx[0:64, c:c + P], ident[0:64, 0:64])
                        last.then_inc(hxtr_done, 1)
                with pe.Else():
                    pe.sem_inc(hxtr_done, 2)
                pe.wait_ge(hgA_ready, 2 * it + 2)
                pe.wait_ge(hgV_ready, 2 * it + 2)
                pe.wait_ge(dispw_ready, 2 * it + 2)
                for a in range(2):
                    for t in range(T):
                        last = nc.tensor.transpose(bank[4][:, (2 * a + t) * P:(2 * a + t + 1) * P],
                                                   dispw[:, t, a * P:a * P + P], ident[:, :])
                last.then_inc(ctr_done, 1)
                for d in range(4):
                    c = 8 + d
                    pe.wait_ge(full[moe_slot(c)], moe_full(it, c))
                    w = cols(moe_slot(c), ID, D)
                    half, i0 = d // 2, (d % 2) * ID
                    for i in range(ID):
                        for h in range(2):
                            last = mm(bank[2][64 * h:64 * h + 64, :],
                                      hg[:, i0 + i, half * BASE:half * BASE + BASE],
                                      w[:, i, h * BANK:h * BANK + BANK],
                                      start=d == 0 and i == 0, stop=d == 3 and i == ID - 1)
                    last.then_inc(down_done, 1)
                    with pe.If(ext > 0):
                        pe.wait_ge(hgxA_ready, it + 1)
                        pe.wait_ge(hgxV_ready, it + 1)
                        for i in range(ID):
                            ii = i0 + i
                            for h in range(2):
                                q = 64 - 64 * h + 32 * (ii % 2)
                                last = mm(bank[3][q:q + 32, :], hgx[:, ii, half * EXT:half * EXT + EXT],
                                          w[:, i, h * BANK:h * BANK + BANK],
                                          start=half == 0 and ii < 2, stop=half == 1 and ii >= NI - 2)
                        last.then_inc(downx_done, 1)
                    with pe.Else():
                        pe.sem_inc(downx_done, 1)

            def final(n):
                ext = pe.value_load(flags[0:1, n:n + 1], min_val=0, max_val=1)
                pe.wait_ge(sc_ready, n + 1)
                pe.wait_ge(y_ready, 2 * n + 2)
                pe.wait_ge(yx_ready, 2 * n + 2)
                pe.wait_ge(xg_ready, 2 * n + 2)
                scatter(ext, n, 0, 6)
                scatter(ext, n, 1, 0)

            gather(1)
            pe.wait_ge(flags_ready, 1)
            pe.wait_ge(zeros_ready, 1)
            with pe.Fori(0, NE, 1) as it:
                expert(it)
            over = pe.value_load(flags[0:1, OVER:OVER + 1], min_val=0, max_val=1)
            with pe.If(over > 0):
                with pe.Fori(NE, NIT, 1) as it:
                    expert(it)
                final(NIT)
            with pe.Else():
                final(NE)


_INS = ["x", "attn_norm", "attn_w_qkv", "attn_sinks", "attn_w_o", "ffn_norm", "ffn_w_gate", "ffn_w_up",
        "ffn_w_down", "pool_norm", "pool_w", "pool_scale", "moe_norm", "moe_w_router", "moe_w_gate",
        "moe_w_up", "moe_w_down", "final_norm"]


def kernel(**inputs):
    import numpy as np
    import concourse.bacc as bacc
    from concourse.bass_utils import run_bass_kernel_spmd

    nc = bacc.Bacc("TRN2", target_bir_lowering=False, num_devices=1)
    arrays, args = {}, []
    for name in _INS:
        a = np.ascontiguousarray(inputs[name])
        arrays[name] = a
        args.append(nc.dram_tensor(name, a.shape, mybir.dt.from_np(a.dtype), kind="ExternalInput").ap())
    args.append(nc.dram_tensor("out", (1, S, D), F32, kind="ExternalOutput").ap())
    trunk_kernel(nc, *args)
    r = run_bass_kernel_spmd(nc, [arrays], core_ids=[0])
    return r.results[0]["out"]
```
